# Optimizing a Trainium2 kernel written in Bass

```python
import jax, jax.numpy as jnp
from jax import lax
import numpy as np

D_MODEL = 1024
BATCH = 1
SEQ = 256
DEPTH = 1
DEC_BATCH = 1
DEC_SEQ = 1024
PAST_LEN = 128

N_MEM = 256
CONV_WIDTH = 768
CONV_K = 3
ATT_HEAD_DIM = 64
DIL_GROUPS = ((128, 1), (512, 4), (2048, 16))
HEADS_PER_GROUP = 4
N_ATT_HEADS = HEADS_PER_GROUP * len(DIL_GROUPS)
ATT_WIDTH = N_ATT_HEADS * ATT_HEAD_DIM
ATT_OUT_WIDTH = HEADS_PER_GROUP * ATT_HEAD_DIM
DIL_BLOCK = 64
XATT_HEADS = 4
XATT_HEAD_DIM = 128
XATT_WIDTH = XATT_HEADS * XATT_HEAD_DIM
N_BRANCH = 3
IN_COLS = 3 * CONV_WIDTH + 3 * ATT_WIDTH + XATT_WIDTH + N_BRANCH * D_MODEL
N_EXPERTS = 16
EC_CAPACITY = 2
D_FF_EXPERT = 1024
ALIBI_MAX_EXP = 8.0
EPS = 1e-6
NEG_INF = -1e30

kernel_name = "hybrid_conv_dilattn_memxattn_ec_encoder"

def rmsnorm(x, g):
    xf = x.astype(jnp.float32)
    y = xf * lax.rsqrt(jnp.mean(xf * xf, axis=-1, keepdims=True) + EPS)
    return (y * g.astype(jnp.float32)).astype(x.dtype)

def alibi_slopes(n):
    return jnp.exp2(-ALIBI_MAX_EXP * jnp.arange(1, n + 1, dtype=jnp.float32) / n)

def short_conv(u, w):
    c = u.shape[-1]
    return lax.conv_general_dilated(
        u, w[:, None, :].astype(u.dtype), window_strides=(1,),
        padding=[(CONV_K // 2, CONV_K // 2)],
        dimension_numbers=("NWC", "WIO", "NWC"), feature_group_count=c)

def dilated_window_attention(q, k, v, dilation, radius, slopes):
    B, S, H, E = q.shape
    L = S // dilation
    nb = -(-L // DIL_BLOCK)
    pad = nb * DIL_BLOCK - L

    def to_sub(t):
        return t.reshape(B, L, dilation, H, E).transpose(0, 2, 1, 3, 4)

    qb = jnp.pad(to_sub(q), ((0, 0), (0, 0), (0, pad), (0, 0), (0, 0)))
    qb = qb.reshape(B, dilation, nb, DIL_BLOCK, H, E)

    def key_windows(t):
        tp = jnp.pad(to_sub(t), ((0, 0), (0, 0), (DIL_BLOCK, pad + DIL_BLOCK), (0, 0), (0, 0)))
        tp = tp.reshape(B, dilation, nb + 2, DIL_BLOCK, H, E)
        return jnp.concatenate([tp[:, :, :-2], tp[:, :, 1:-1], tp[:, :, 2:]], axis=3)

    kw = key_windows(k)
    vw = key_windows(v)

    blk = jnp.arange(nb)[:, None, None]
    a = jnp.arange(DIL_BLOCK)[None, :, None]
    c = jnp.arange(3 * DIL_BLOCK)[None, None, :]
    delta = c - DIL_BLOCK - a
    kpos = (blk - 1) * DIL_BLOCK + c
    valid = (jnp.abs(delta) <= radius) & (kpos >= 0) & (kpos < L)
    dist = (dilation * jnp.abs(delta[0])).astype(jnp.float32)
    bias = -slopes[:, None, None] * dist[None]

    s = jnp.einsum("bdnqhe,bdnkhe->bdnhqk", qb, kw).astype(jnp.float32) * (E ** -0.5)
    s = jnp.where(valid[None, None, :, None], s + bias, NEG_INF)
    lse = jax.nn.logsumexp(s, axis=-1)
    p = jnp.exp(s - lse[..., None]).astype(v.dtype)
    o = jnp.einsum("bdnhqk,bdnkhe->bdnqhe", p, vw)
    o = o.reshape(B, dilation, nb * DIL_BLOCK, H, E)[:, :, :L]
    o = o.transpose(0, 2, 1, 3, 4).reshape(B, S, H, E)
    lse = lse.transpose(0, 1, 2, 4, 3).reshape(B, dilation, nb * DIL_BLOCK, H)[:, :, :L]
    lse = lse.transpose(0, 2, 1, 3).reshape(B, S, H)
    return o, lse

def dilated_mixture_attention(q, k, v, q_g, k_g):
    B, S, _ = q.shape
    q = rmsnorm(q.reshape(B, S, N_ATT_HEADS, ATT_HEAD_DIM), q_g)
    k = rmsnorm(k.reshape(B, S, N_ATT_HEADS, ATT_HEAD_DIM), k_g)
    v = v.reshape(B, S, N_ATT_HEADS, ATT_HEAD_DIM)
    slopes = alibi_slopes(N_ATT_HEADS)
    outs, lses = [], []
    for g, (window, dilation) in enumerate(DIL_GROUPS):
        hs = slice(g * HEADS_PER_GROUP, (g + 1) * HEADS_PER_GROUP)
        radius = window // (2 * dilation)
        o, lse = dilated_window_attention(q[:, :, hs], k[:, :, hs], v[:, :, hs],
                                          dilation, radius, slopes[hs])
        outs.append(o)
        lses.append(lse)
    w = jax.nn.softmax(jnp.stack(lses, axis=0), axis=0)
    o = jnp.sum(w[..., None] * jnp.stack(outs, axis=0).astype(jnp.float32), axis=0)
    return o.astype(q.dtype).reshape(B, S, ATT_OUT_WIDTH)

def memory_cross_attention(xq, mem, mem_g, w_mem_kv, xq_g, xk_g):
    B, S, _ = xq.shape
    M = mem.shape[1]
    q = rmsnorm(xq.reshape(B, S, XATT_HEADS, XATT_HEAD_DIM), xq_g)
    kv = rmsnorm(mem, mem_g) @ w_mem_kv
    k, v = jnp.split(kv, 2, axis=-1)
    k = rmsnorm(k.reshape(B, M, XATT_HEADS, XATT_HEAD_DIM), xk_g)
    v = v.reshape(B, M, XATT_HEADS, XATT_HEAD_DIM)
    s = jnp.einsum("bshe,bmhe->bhsm", q, k).astype(jnp.float32) * (XATT_HEAD_DIM ** -0.5)
    p = jax.nn.softmax(s, axis=-1).astype(v.dtype)
    return jnp.einsum("bhsm,bmhe->bshe", p, v).reshape(B, S, XATT_WIDTH)

def expert_choice_ffn(h, w_router, w_gate, w_up, w_down):
    B, S, D = h.shape
    n_tok = B * S
    t = h.reshape(n_tok, D)
    aff = jax.nn.softmax((t @ w_router).astype(jnp.float32), axis=-1)
    cap = max(1, EC_CAPACITY * n_tok // N_EXPERTS)
    gate, idx = lax.top_k(aff.T, cap)
    xe = jnp.take(t, idx, axis=0)
    hid = jax.nn.silu(jnp.einsum("ecd,edf->ecf", xe, w_gate)) * jnp.einsum("ecd,edf->ecf", xe, w_up)
    ye = jnp.einsum("ecf,efd->ecd", hid, w_down) * gate[..., None].astype(h.dtype)
    out = jnp.zeros_like(t).at[idx.reshape(-1)].add(ye.reshape(-1, D))
    return out.reshape(B, S, D)

def encoder_layer(x, mem, norm1_g, w_in, conv_w, q_norm_g, k_norm_g, mem_norm_g, w_mem_kv,
                  xq_norm_g, xk_norm_g, w_br_conv, w_br_attn, w_br_xattn, w_o, norm2_g,
                  w_router, w_exp_gate, w_exp_up, w_exp_down):
    B, S, D = x.shape
    h = rmsnorm(x, norm1_g)
    proj = h @ w_in
    sizes = [CONV_WIDTH] * 3 + [ATT_WIDTH] * 3 + [XATT_WIDTH, N_BRANCH * D_MODEL]
    cuts = [int(c) for c in np.cumsum(sizes)[:-1]]
    cb, cc, cx, aq, ak, av, xq, gates = jnp.split(proj, cuts, axis=-1)

    y_conv = (cb * short_conv(cc * cx, conv_w)) @ w_br_conv
    y_attn = dilated_mixture_attention(aq, ak, av, q_norm_g, k_norm_g) @ w_br_attn
    y_x = memory_cross_attention(xq, mem, mem_norm_g, w_mem_kv, xq_norm_g, xk_norm_g) @ w_br_xattn

    g = jax.nn.sigmoid(gates.astype(jnp.float32)).astype(x.dtype).reshape(B, S, N_BRANCH, D)
    merged = g[:, :, 0] * y_conv + g[:, :, 1] * y_attn + g[:, :, 2] * y_x
    x = x + merged @ w_o

    x = x + expert_choice_ffn(rmsnorm(x, norm2_g), w_router, w_exp_gate, w_exp_up, w_exp_down)
    return x

def setup_inputs(seed: int = 0) -> dict:
    key = jax.random.key(seed)
    ks = jax.random.split(key, 24)
    f32 = jnp.float32

    def nrm(k, shape, fan_in):
        return jax.random.normal(k, shape, f32) * (fan_in ** -0.5)

    def gain(k, shape):
        return 1.0 + 0.02 * jax.random.normal(k, shape, f32)

    L = DEPTH
    return {
        "x_prompt": jax.random.normal(ks[0], (BATCH, SEQ, D_MODEL), f32),
        "x_sample": jax.random.normal(ks[1], (DEC_BATCH, DEC_SEQ, D_MODEL), f32),
        "mem_prompt": jax.random.normal(ks[2], (BATCH, N_MEM, D_MODEL), f32),
        "mem_sample": jax.random.normal(ks[3], (DEC_BATCH, N_MEM, D_MODEL), f32),
        "norm1_g": gain(ks[4], (L, D_MODEL)),
        "w_in": nrm(ks[5], (L, D_MODEL, IN_COLS), D_MODEL),
        "conv_w": nrm(ks[6], (L, CONV_K, CONV_WIDTH), CONV_K),
        "q_norm_g": gain(ks[7], (L, ATT_HEAD_DIM)),
        "k_norm_g": gain(ks[8], (L, ATT_HEAD_DIM)),
        "mem_norm_g": gain(ks[9], (L, D_MODEL)),
        "w_mem_kv": nrm(ks[10], (L, D_MODEL, 2 * XATT_WIDTH), D_MODEL),
        "xq_norm_g": gain(ks[11], (L, XATT_HEAD_DIM)),
        "xk_norm_g": gain(ks[12], (L, XATT_HEAD_DIM)),
        "w_br_conv": nrm(ks[13], (L, CONV_WIDTH, D_MODEL), CONV_WIDTH),
        "w_br_attn": nrm(ks[14], (L, ATT_OUT_WIDTH, D_MODEL), ATT_OUT_WIDTH),
        "w_br_xattn": nrm(ks[15], (L, XATT_WIDTH, D_MODEL), XATT_WIDTH),
        "w_o": nrm(ks[16], (L, D_MODEL, D_MODEL), D_MODEL),
        "norm2_g": gain(ks[17], (L, D_MODEL)),
        "w_router": nrm(ks[18], (L, D_MODEL, N_EXPERTS), D_MODEL),
        "w_exp_gate": nrm(ks[19], (L, N_EXPERTS, D_MODEL, D_FF_EXPERT), D_MODEL),
        "w_exp_up": nrm(ks[20], (L, N_EXPERTS, D_MODEL, D_FF_EXPERT), D_MODEL),
        "w_exp_down": nrm(ks[21], (L, N_EXPERTS, D_FF_EXPERT, D_MODEL), D_FF_EXPERT),
    }

def reference(x_prompt, x_sample, mem_prompt, mem_sample, norm1_g, w_in, conv_w, q_norm_g,
              k_norm_g, mem_norm_g, w_mem_kv, xq_norm_g, xk_norm_g, w_br_conv, w_br_attn,
              w_br_xattn, w_o, norm2_g, w_router, w_exp_gate, w_exp_up, w_exp_down):
    y_prompt = x_prompt
    y_sample = x_sample
    for l in range(DEPTH):
        p = (norm1_g[l], w_in[l], conv_w[l], q_norm_g[l], k_norm_g[l], mem_norm_g[l], w_mem_kv[l],
             xq_norm_g[l], xk_norm_g[l], w_br_conv[l], w_br_attn[l], w_br_xattn[l], w_o[l],
             norm2_g[l], w_router[l], w_exp_gate[l], w_exp_up[l], w_exp_down[l])
        y_prompt = encoder_layer(y_prompt, mem_prompt, *p)
        y_sample = encoder_layer(y_sample, mem_sample, *p)
    return (y_prompt, y_sample)


_drawn_inputs = setup_inputs


def setup_inputs(seed=0):
    import zlib

    import numpy as np

    out = dict(_drawn_inputs(seed))
    spreads = {}
    factors = {'q_norm_g': 6.892,
     'k_norm_g': 7.583,
     'mem_norm_g': 8.0,
     'xq_norm_g': 8.0,
     'xk_norm_g': 8.0,
     'norm2_g': 3.725}
    for name, (base, spread) in spreads.items():
        noise = np.random.default_rng([zlib.crc32(name.encode()), seed]).standard_normal(out[name].shape)
        drawn = base * np.exp(spread * noise) if base else spread * noise
        out[name] = __import__('jax').numpy.asarray(drawn.astype(out[name].dtype))
    for name, factor in factors.items():
        out[name] = (out[name] * factor).astype(out[name].dtype)
    return out
```

```python
from contextlib import ExitStack

import concourse.bass as bass
from concourse import mybir

F32 = mybir.dt.float32
F32R = mybir.dt.float32r
I32 = mybir.dt.int32
U32 = mybir.dt.uint32
ALU = mybir.AluOpType
ACT = mybir.ActivationFunctionType
AX = mybir.AxisListType

P = 128
D = 1024
KD = D // P
NP_, NS_ = 256, 1024
NT = NP_ + NS_
NMEM = 512
CW = 768
NCC = CW // P
E_ATT = 64
NH = 12
E_X = 128
XH = 4
NEXP = 16
FF = 1024
CAP_P, CAP_S = 2 * NP_ // NEXP, 2 * NS_ // NEXP
CAP = CAP_P + CAP_S
EPS = 1e-6
BIG = 1e30
SEGS = ((0, 256), (256, 512), (768, 512))
COL_Q, COL_K, COL_V = 3 * CW, 3 * CW + NH * E_ATT, 3 * CW + 2 * NH * E_ATT
COL_X = 3 * CW + 3 * NH * E_ATT
COL_G = COL_X + XH * E_X


def tiles_of(group):
    vtiles, tiles = [], []

    def windowed(base, stride, length):
        first = len(vtiles)
        edges = [0] + list(range(64, length, 128)) + [length]
        for a, b in zip(edges, edges[1:]):
            vtiles.append((base + stride * a, stride, b - a))
        for t in range(length // P):
            keys = [first + t, first + t + 1]
            tiles.append((base + stride * P * t, stride, keys, "window", 64 if t == 0 else 0))

    def whole(base, stride, kind):
        vtiles.append((base, stride, P))
        tiles.append((base, stride, [len(vtiles) - 1], kind, 0))

    if group == 0:
        windowed(0, 1, NP_)
        windowed(NP_, 1, NS_)
    elif group == 1:
        for c in range(2):
            whole(c, 2, "par2")
        for c in range(4):
            windowed(NP_ + c, 4, NS_ // 4)
    else:
        for c in range(2):
            whole(c, 2, "par8")
        for c in range(8):
            whole(NP_ + c, 8, "par2")
    return vtiles, tiles


GEO = [tiles_of(g) for g in range(3)]
DILATION = (1, 4, 16)


def slope(head):
    return 2.0 ** (-8.0 * (head + 1) / NH)


def plan():
    chunks, segs = [], []

    def chunk(src, col, kind, place, over):
        c = len(chunks)
        chunks.append((src, col))
        for n, (t0, nt) in enumerate(over):
            segs.append(dict(chunk=c, first=n == 0, last=n == len(over) - 1, kind=kind, place=place,
                             t0=t0, nt=nt, mem=src == "mem"))

    for j in range(XH):
        chunk("mem", j * P, "k", ("memk", j), ((0, NMEM),))
    for j in range(XH):
        chunk("mem", (XH + j) * P, "v", ("memv", j), ((0, NMEM),))
    for ph in range(6):
        pair, g = ph // 3, ph % 3
        off = g * 4 * E_ATT + pair * P
        chunk("in", COL_Q + off, "q", ("q", ph), SEGS)
        chunk("in", COL_K + off, "k", ("k", ph), SEGS)
        chunk("in", COL_V + off, "v", ("v", ph), SEGS)
    for j in range(XH):
        chunk("in", COL_X + j * P, "q", ("xq", j), SEGS)
    return chunks, segs


def units_of():
    units = []
    for ph in range(6):
        for t in range(10):
            units.append(("att", ph, t))
    for j in range(XH):
        for t in range(5):
            units.append(("mem", j, t))
    return units


def kernel_body(nc, x, mem, g1, gm, gq, gk, gxq, gxk, convw, w_in, w_mem, w_bc, w_ba, w_bx, w_o, g2, w_r,
                w_eg, w_eu, w_ed, y):
    ctx = ExitStack()
    BASE = 16512
    LIMIT = 229344

    def at(name, shape, dt, offset):
        size = 4
        for s in shape[1:]:
            size *= s
        assert BASE + offset + size <= LIMIT, (name, BASE + offset + size)
        return nc.alloc_sbuf_tensor_at(name, shape, dt, offset=BASE + offset)

    def sem(name):
        return ctx.enter_context(nc.semaphore(name))

    chunks, segs = plan()
    units = units_of()
    NSEG = len(segs)

    o = 0

    def small(name, n, dt=F32, parts=P):
        nonlocal o
        t = at(name, [parts, n], dt, o)
        o += -(-4 * n // 32) * 32
        return t

    ident = small("ident", P)
    ones = small("ones", P)
    pair_ones = small("pair_ones", P)
    head_rows = small("head_rows", P, parts=2)
    dist_win = small("dist_win", 256)
    dist_par2 = small("dist_par2", P)
    dist_par8 = small("dist_par8", P)
    g1c = small("g1c", KD)
    gmc = small("gmc", KD)
    gqc = small("gqc", 1)
    gkc = small("gkc", 1)
    gxqc = small("gxqc", 1)
    gxkc = small("gxkc", 1)
    cwc = small("cwc", 3 * NCC)
    eps_d = small("eps_d", 1)
    eps_a = small("eps_a", 1)
    eps_x = small("eps_x", 1)
    sumsq = small("sumsq", 16)
    rstd = small("rstd", 16)
    L_ = small("row_sum", 6)
    lnL = small("ln_sum", 6)
    rL = small("inv_sum", 6)
    nmax = small("neg_max", 6)
    lse = small("lse", 6)
    assert o <= 6400, o
    HT = 6400
    hT_hi = at("hT_hi", [P, KD, NT], F32R, HT)
    hT_lo = at("hT_lo", [P, KD, NT], F32R, HT + 40960)
    RING = HT + 81920
    NRAW, NSPL = 3, 2
    raw = [at(f"raw{i}", [P, KD, P], F32, RING + 4096 * i) for i in range(NRAW)]
    whi = [at(f"whi{i}", [P, KD, P], F32R, RING + 12288 + 4096 * i) for i in range(NSPL)]
    wlo = [at(f"wlo{i}", [P, KD, P], F32R, RING + 20480 + 4096 * i) for i in range(NSPL)]
    OB = RING + 28672
    oB = at("oB", [P, 2, NT], F32, OB)
    vsum = at("vsum", [2, NT], F32, OB + 5120)
    W = OB + 10240
    OT = at("OT", [P, 3, NT], F32, W)
    LS = at("LS", [2, 3, NT], F32, W + 15360)
    oC = at("oC", [P, XH, NT], F32, W)
    qT = [at(f"qT{i}", [P, NT], F32, W + 30720 + 5120 * i) for i in range(2)]
    kT = [at(f"kT{i}", [P, NT], F32, W + 40960 + 5120 * i) for i in range(2)]
    V = [at(f"V{i}", [P, 14, P], F32, W + 51200 + 7168 * i) for i in range(2)]
    vT = at("vT", [P, NT], F32, W + 65536)
    sq = [at(f"sq{i}", [P, 512], F32, W + 70656 + 2048 * i) for i in range(2)]
    Pm = [at(f"Pm{i}", [P, 2, 256], F32, W + 74752 + 2048 * i) for i in range(3)]
    PT = [at(f"PT{i}", [P, 4, P], F32, W + 80896 + 2048 * i) for i in range(2)]
    memT_hi = at("memT_hi", [P, KD, NMEM], F32R, W)
    memT_lo = at("memT_lo", [P, KD, NMEM], F32R, W + 16384)
    Kx_early = at("Kx_early", [P, XH, NMEM], F32, W + 32768 + 2048 + 1024)
    Vx_early = at("Vx_early", [P, 4, XH * P], F32, W + 57344)
    Kx = at("Kx", [P, XH, NMEM], F32, W + 40960)
    Vx = at("Vx", [P, 4, XH * P], F32, W + 49152)
    xq = [qT[0], vT, qT[1], at("xq3", [P, NT], F32, W + 57344)]
    scratch_kx = nc.dram_tensor("scratch_kx", [P, XH * NMEM], F32, kind="Internal").ap()
    scratch_vx = nc.dram_tensor("scratch_vx", [P, 4 * XH * P], F32, kind="Internal").ap()
    scratch_m = nc.dram_tensor("scratch_m", [KD, P, NT], F32, kind="Internal").ap()
    scratch_t = nc.dram_tensor("scratch_t", [NT, D], F32, kind="Internal").ap()

    pairs = [ctx.enter_context(nc.psum_tensor(f"bank_pair{i}", [P, 2, 512], F32)) for i in range(4)]
    bank = [pairs[i // 2][:, i % 2, :] for i in range(6)]
    pair_bank = pairs[3]

    s_const = sem("const_loaded")
    s_ident = sem("consts_made")
    s_dist = sem("distances")
    s_dchain = sem("distances_step")
    s_xin = [sem(f"x_loaded{i}") for i in range(2)]
    s_ss = sem("x_squares")
    s_rs = sem("x_rstd")
    s_xn = sem("x_normed")
    s_tr = sem("x_transposed")
    s_tg = sem("x_gained")
    s_hi = sem("x_hi")
    s_lo = sem("x_lo")
    xt = [at(f"xt{i}", [P, D], F32, W + 32768 + 4096 * i) for i in range(2)]
    xn = [at(f"xn{i}", [P, D], F32, W + 40960 + 4096 * i) for i in range(2)]
    tg = [at(f"tg{i}", [P, KD, P], F32, W + 49152 + 4096 * i) for i in range(2)]
    junk = at("junk", [P, D], F32, W + 57344)
    dwork = at("dwork", [P, 3, 256], F32, W + 61440)
    diwork = at("diwork", [P, 2, 128], I32, W + 64512)

    tile_src = [("x", i) for i in range(NT // P)] + [("m", i) for i in range(NMEM // P)]
    NTILE = len(tile_src)

    raw_loaded = [sem(f"raw_loaded{i}") for i in range(NRAW)]
    hi_ready = sem("whi_ready")
    lo_ready = sem("wlo_ready")

    n_straight = len(chunks)

    C_CONV = n_straight
    C_GATE = C_CONV + 3 * NCC
    C_END = C_GATE + 3 * KD
    CONV_COLS = (CW, 2 * CW, 0)

    def cols_of(w, col):
        return w[:, bass.ds(col, P)].rearrange("(k p) n -> p k n", p=P)

    def conv_src(ch, part):
        return cols_of(w_in, CONV_COLS[part] + P * ch)

    def gate_src(m, b):
        return cols_of(w_in, COL_G + D * b + P * m)

    def chunk_src(c):
        if c >= C_GATE:
            return gate_src((c - C_GATE) // 3, (c - C_GATE) % 3)
        if c >= C_CONV:
            return conv_src((c - C_CONV) // 3, (c - C_CONV) % 3)
        src, col = chunks[c]
        return cols_of(w_mem if src == "mem" else w_in, col)

    with nc.Block() as block:
        @block.sync
        def _(sp):
            ctx.enter_context(nc.allow_non_contiguous_dma(reason="a few vectors"))
            sp.dma_start(g1c[:], g1.rearrange("(k p) -> p k", p=P)).then_inc(s_const, 16)
            sp.dma_start(gmc[:], gm.rearrange("(k p) -> p k", p=P)).then_inc(s_const, 16)
            for h in range(2):
                sp.dma_start(gqc[64 * h:64 * h + 64, :], gq.rearrange("(p a) -> p a", a=1)).then_inc(s_const, 16)
                sp.dma_start(gkc[64 * h:64 * h + 64, :], gk.rearrange("(p a) -> p a", a=1)).then_inc(s_const, 16)
            sp.dma_start(gxqc[:], gxq.rearrange("(p a) -> p a", a=1)).then_inc(s_const, 16)
            sp.dma_start(gxkc[:], gxk.rearrange("(p a) -> p a", a=1)).then_inc(s_const, 16)
            sp.dma_start(cwc[:].rearrange("p (j c) -> p j c", j=3),
                         convw.rearrange("j (c p) -> p j c", p=P)).then_inc(s_const, 16)
            for n, (src, i) in enumerate(tile_src):
                if n >= 2:
                    sp.wait_ge(s_xn, n - 1)
                a = (x if src == "x" else mem)[i * P:(i + 1) * P, :]
                sp.dma_start(xt[n % 2][:], a).then_inc(s_xin[n % 2], 16)
            for c in range(NRAW):
                sp.dma_start(raw[c][:], chunk_src(c)).then_inc(raw_loaded[c], 16)

        @block.gpsimd
        def _(pool):
            pool.memset(ident[:], 0.0).then_inc(s_ident, 1)
            pool.memset(ones[:], 1.0)
            pool.memset(head_rows[:], 1.0)
            pool.memset(eps_d[:], EPS)
            pool.memset(eps_a[:], EPS * E_ATT)
            pool.memset(eps_x[:], EPS * E_X).then_inc(s_ident, 1)
            pool.wait_ge(s_ident, 2)
            pool.affine_select(out=ident[:], in_=ident[:], compare_op=ALU.not_equal, fill=1.0, base=0,
                               pattern=[[-1, P]], channel_multiplier=1).then_inc(s_ident, 1)
            pool.affine_select(out=head_rows[:], in_=head_rows[:], compare_op=ALU.is_ge, fill=0.0, base=0,
                               pattern=[[1, P]], channel_multiplier=-64).then_inc(s_ident, 1)
            pool.wait_ge(s_ident, 4)
            pool.affine_select(out=head_rows[:], in_=head_rows[:], compare_op=ALU.is_ge, fill=0.0, base=63,
                               pattern=[[-1, P]], channel_multiplier=64).then_inc(s_ident, 1)
            pool.iota(dwork[:, 0, :], [[1, 256]], base=-64, channel_multiplier=-1,
                      allow_small_or_imprecise_dtypes=True)
            pool.iota(dwork[:, 1, 0:P], [[1, P]], base=0, channel_multiplier=-1,
                      allow_small_or_imprecise_dtypes=True)
            pool.iota(diwork[:, 0, :], [[1, P]], base=0, channel_multiplier=-1).then_inc(s_dist, 1)
            pool.wait_ge(s_dist, 2)
            pool.affine_select(out=dist_win[:], in_=dist_win[:], compare_op=ALU.is_ge, fill=BIG, base=128,
                               pattern=[[-1, 256]], channel_multiplier=1).then_inc(s_dist, 1)
            pool.wait_ge(s_dist, 3)
            pool.affine_select(out=dist_win[:], in_=dist_win[:], compare_op=ALU.is_ge, fill=BIG, base=0,
                               pattern=[[1, 256]], channel_multiplier=-1).then_inc(s_dist, 1)

        @block.scalar
        def _(act):
            nc.scalar.preload_act_table_set("natural_log_exp_and_others")
            act.wait_ge(s_ident, 2)
            for n in range(NTILE + 1):
                if n < NTILE:
                    act.wait_ge(s_xin[n % 2], 16 * (n // 2 + 1))
                    if n >= 1:
                        act.wait_ge(s_rs, 2 * n)
                    nc.scalar.activation(junk[:], xt[n % 2][:], ACT.Square,
                                         accum_out=sumsq[:, n:n + 1]).then_inc(s_ss, 1)
                    act.wait_ge(s_ss, n + 1)
                    nc.scalar.activation(rstd[:, n:n + 1], sumsq[:, n:n + 1], ACT.Ln, bias=eps_d[:, 0:1],
                                         scale=1.0 / D).then_inc(s_rs, 1)
                    act.wait_ge(s_rs, 2 * n + 1)
                    nc.scalar.activation(rstd[:, n:n + 1], rstd[:, n:n + 1], ACT.Exp,
                                         scale=-0.5).then_inc(s_rs, 1)
                if n >= 1:
                    m = n - 1
                    act.wait_ge(s_tg, m + 1)
                    dst, i = (hT_hi, m) if m < 10 else (memT_hi, m - 10)
                    nc.scalar.activation(dst[:, :, i * P:(i + 1) * P], tg[m % 2][:],
                                         ACT.Copy).then_inc(s_hi, 1)

        @block.vector
        def _(dve):
            steps = [0]

            def step(ins):
                steps[0] += 1
                ins.then_inc(s_dchain, 1)
                dve.wait_ge(s_dchain, steps[0])

            for a in range(2):
                for b in range(2):
                    nc.vector.memset(pair_ones[64 * a:64 * a + 64, 64 * b:64 * b + 64], float(a == b))
            dve.wait_ge(s_dist, 1)
            step(nc.vector.tensor_scalar(dwork[:, 2, :], dwork[:, 0, :], -1.0, None, ALU.mult))
            nc.vector.tensor_tensor(dist_win[:], dwork[:, 0, :], dwork[:, 2, :], ALU.max).then_inc(s_dist, 1)
            dve.wait_ge(s_dist, 2)
            step(nc.vector.tensor_scalar(dwork[:, 2, 0:P], dwork[:, 1, 0:P], -1.0, None, ALU.mult))
            step(nc.vector.tensor_tensor(dwork[:, 0, 0:P], dwork[:, 1, 0:P], dwork[:, 2, 0:P], ALU.max))
            for mask, out in ((1, dist_par2), (7, dist_par8)):
                step(nc.vector.tensor_scalar(diwork[:, 1, :], diwork[:, 0, :], mask, None, ALU.bitwise_and))
                step(nc.vector.tensor_copy(dwork[:, 1, 0:P], diwork[:, 1, :]))
                step(nc.vector.tensor_scalar(dwork[:, 2, 0:P], dwork[:, 1, 0:P], BIG, None, ALU.mult))
                step(nc.vector.scalar_tensor_tensor(out[:], dwork[:, 0, 0:P], 1.0 / (mask + 1), dwork[:, 2, 0:P],
                                                    ALU.mult, ALU.add))
            dve.wait_ge(s_const, 16 * 9)
            step(nc.vector.tensor_scalar(gkc[:], gkc[:], float(E_ATT) ** 0.5, None, ALU.mult))
            step(nc.vector.tensor_scalar(gxkc[:], gxkc[:], float(E_X) ** 0.5, None, ALU.mult))
            for n in range(NTILE + 1):
                if n < NTILE:
                    dve.wait_ge(s_rs, 2 * n + 2)
                    if n >= 2:
                        dve.wait_ge(s_xn, n - 1)
                        dve.wait_ge(s_tr, n - 1)
                    nc.vector.tensor_scalar(xn[n % 2][:], xt[n % 2][:], rstd[:, n:n + 1], None,
                                            ALU.mult).then_inc(s_xn, 1)
                if n >= 1:
                    m = n - 1
                    dve.wait_ge(s_tr, m + 1)
                    if m >= 2:
                        dve.wait_ge(s_lo, m - 1)
                        dve.wait_ge(s_hi, m - 1)
                    gc = g1c if m < 10 else gmc
                    src = (bank[0:2], bank[2:4])[m % 2]
                    for h in range(2):
                        ins = nc.vector.tensor_tensor(
                            tg[m % 2][:, 4 * h:4 * h + 4, :], src[h][:].rearrange("p (k t) -> p k t", k=4),
                            gc[:, 4 * h:4 * h + 4].unsqueeze(2).to_broadcast([P, 4, P]), ALU.mult)
                    ins.then_inc(s_tg, 1)
                    dve.wait_ge(s_tg, m + 1)
                    dve.wait_ge(s_hi, m + 1)
                    hi, lo, i = (hT_hi, hT_lo, m) if m < 10 else (memT_hi, memT_lo, m - 10)
                    nc.vector.tensor_tensor(lo[:, :, i * P:(i + 1) * P], tg[m % 2][:],
                                            hi[:, :, i * P:(i + 1) * P].bitcast(F32),
                                            ALU.subtract).then_inc(s_lo, 1)

        @block.tensor
        def _(pe):
            pe.wait_ge(s_ident, 3)
            for n in range(NTILE):
                pe.wait_ge(s_xn, n + 1)
                if n >= 2:
                    pe.wait_ge(s_tg, n - 1)
                dst = (bank[0:2], bank[2:4])[n % 2]
                for k in range(KD):
                    ins = nc.tensor.transpose(dst[k // 4][:, (k % 4) * P:(k % 4 + 1) * P],
                                              xn[n % 2][:, k * P:(k + 1) * P], ident[:])
                ins.then_inc(s_tr, 1)

    seg_done = sem("seg_done")
    seg_free = sem("seg_free")
    sq_ready = sem("sq_ready")
    ss_done = sem("ss_done")
    lnexp = sem("lnexp")
    sc_done = sem("scores_done")
    mx_done = sem("max_done")
    ex_done = sem("exp_done")
    s_inv = sem("inv_sum_ready")
    s_lse = sem("lse_ready")
    p_norm = sem("probs_normed")
    tp_done = sem("probs_transposed")
    pt_done = sem("pt_copied")
    ls_done = sem("lse_transposed")
    ls_copied = sem("lse_copied")
    pv_done = sem("pv_done")
    o_copied = sem("o_copied")
    a_chain = sem("act_step")
    d_chain = sem("dve_step")
    s_memout = sem("mem_kv_saved")
    s_memin = sem("mem_kv_loaded")
    s_vtr = sem("v_transposed")
    s_vcp = sem("v_copied")
    c_dsub = sem("combine_differences")
    c_exp = sem("combine_exps")
    c_sum = sem("combine_sum")
    c_inv = sem("combine_inverse")
    c_w = sem("combine_weights")
    c_bc = sem("weights_broadcast")
    c_bu = sem("broadcast_used")
    c_done = sem("combined")

    s_bank = (pair_bank[:, 0, :], pair_bank[:, 1, :])
    misc, tbank, obank = bank[3], bank[4], bank[5]
    w_bank = (misc, *s_bank)
    norm_segs = [s for s in range(NSEG) if segs[s]["kind"] != "v"]
    norm_no = {s: n for n, s in enumerate(norm_segs)}
    last_seg = {sg["chunk"]: s for s, sg in enumerate(segs)}

    def v_rounds(place):
        kind, n = place
        if kind == "memv":
            return [[(t, P * t, 1, P) for t in range(4)]]
        vt = [(i, a, st, ln) for i, (a, st, ln) in enumerate(GEO[n % 3][0])]
        return [vt[i:i + 4] for i in range(0, len(vt), 4)]

    EXTRA = 14
    ticks = [dict(seg=s if s < NSEG else None, units=[], rounds=[], combine=[], amid=[], after=[])
             for s in range(NSEG + EXTRA)]
    order = {sg["place"]: s for s, sg in enumerate(segs) if sg["last"]}
    for s, sg in enumerate(segs):
        if sg["kind"] == "v" and sg["last"]:
            for i, r in enumerate(v_rounds(sg["place"])):
                ticks[s + 1 + i // 2]["rounds"].append((sg["place"], r))
    n_units = len(units)
    for ph in range(6):
        start = order[("v", ph)] + 3 + 2 * (ph == 3)
        room = {3: 5, 5: 4}.get(ph, 7)
        for i in range(10):
            ticks[start + i * room // 10]["units"].append(10 * ph + i)
        if ph % 3 == 2:
            for i in range(4):
                ticks[start + room + 1 + i]["combine"].append((ph // 3, i))
            after = start + room + 5
    for i in range(n_units - 60):
        ticks[after + i // 5]["units"].append(60 + i)
    scored, transposed = [], []
    for tk in ticks:
        for n, v in enumerate(tk["units"] or [None]):
            acts = tk["amid" if n == 0 and tk["seg"] is not None else "after"]
            ready = transposed[:]
            transposed.clear()
            if v is not None:
                scored.append(v)
            u = scored.pop(0) if scored and (v is None or len(scored) > 2) else None
            if u is not None and u < 60:
                acts.append(("lse", u))
            if v is not None:
                acts.append(("scores", v))
            if u is not None:
                acts.append(("transposes", u))
                transposed.append(u)
            acts += [("values", w) for w in ready]
    assert not scored and not transposed

    t_use, use_no, round_list = [], {}, []
    for tk in ticks:
        uses = [("u", v) for what, v in tk["amid"] if what == "transposes"]
        for r in tk["rounds"]:
            uses.append(("v", len(round_list)))
            round_list.append(r)
        uses += [("u", v) for what, v in tk["after"] if what == "transposes"]
        for use in uses:
            use_no[use] = len(t_use)
            t_use.append(use)

    att_units = [v for v in range(n_units) if units[v][0] == "att"]
    N_ATT = len(att_units)

    def unit(v):
        kind, n, t = units[v]
        if kind == "att":
            vt, tl = GEO[n % 3]
            base, st, keys, bias, boff = tl[t]
            kk = [(i, *vt[i]) for i in keys]
            return dict(att=True, ph=n, g=n % 3, pair=n // 3, base=base, st=st, keys=kk, bias=bias, boff=boff,
                        nk=sum(k[3] for k in kk), buf=n % 2)
        return dict(att=False, j=n, t=t, buf=n % 2, nk=256)

    def tok(t, base, st, n=P):
        return slice(base, base + st * (n - 1) + 1, st) if st > 1 else slice(base, base + n)

    def wait_rounds_done(eng, place):
        n = max(i for i, (pl, _) in enumerate(round_list) if pl == place)
        eng.wait_ge(s_vcp, n + 1)

    with nc.Block() as block:
        @block.sync
        def _(sp):
            for c in range(NRAW, n_straight + NRAW):
                sp.wait_ge(lo_ready, c - NRAW + 1)
                if c < C_END:
                    sp.dma_start(raw[c % NRAW][:], chunk_src(c)).then_inc(raw_loaded[c % NRAW], 16)
                if c == 11:
                    sp.wait_ge(seg_free, 8)
                    sp.wait_ge(s_vcp, 4)
                    sp.dma_start(scratch_kx, Kx_early[:].rearrange("p a b -> p (a b)")).then_inc(s_memout, 16)
                    sp.dma_start(scratch_vx, Vx_early[:].rearrange("p a b -> p (a b)")).then_inc(s_memout, 16)
            sp.wait_ge(s_memout, 32)
            sp.wait_ge(pv_done, N_ATT)
            sp.dma_start(Kx[:].rearrange("p a b -> p (a b)"), scratch_kx).then_inc(s_memin, 16)
            sp.dma_start(Vx[:].rearrange("p a b -> p (a b)"), scratch_vx).then_inc(s_memin, 16)

        @block.scalar
        def _(act):
            steps = [0]

            def step(ins):
                steps[0] += 1
                ins.then_inc(a_chain, 1)
                act.wait_ge(a_chain, steps[0])

            def split_hi(c):
                act.wait_ge(raw_loaded[c % NRAW], 16 * (c // NRAW + 1))
                if c >= NSPL:
                    act.wait_ge(seg_done, last_seg[c - NSPL] + 1)
                nc.scalar.activation(whi[c % NSPL][:], raw[c % NRAW][:], ACT.Copy).then_inc(hi_ready, 1)

            def o_copy(v):
                un = unit(v)
                act.wait_ge(pv_done, v + 1)
                if un["att"]:
                    dst = OT[:, un["g"], tok(None, un["base"], un["st"])]
                    if un["g"] == 0 and un["pair"] == 1 and units[v][2] == 0:
                        act.wait_ge(c_done, 1)
                    nc.scalar.activation(dst, obank[:, 0:P], ACT.Copy).then_inc(o_copied, 1)
                else:
                    act.wait_ge(c_done, 2)
                    nc.scalar.activation(oC[:, un["j"], 2 * P * un["t"]:2 * P * (un["t"] + 1)],
                                         obank[:, 0:2 * P], ACT.Copy).then_inc(o_copied, 1)

            def exps(v):
                un = unit(v)
                act.wait_ge(mx_done, v + 1)
                pm, nk, b = Pm[v % 3], un["nk"], 2 * (v % 3)
                if v >= 3:
                    act.wait_ge(p_norm, v - 2)
                for h in range(2):
                    src = pm[:, h, 0:nk] if un["att"] else s_bank[h][:, 0:nk]
                    ins = nc.scalar.activation(pm[:, h, 0:nk], src, ACT.Exp, bias=nmax[:, b + h:b + h + 1],
                                               accum_out=L_[:, b + h:b + h + 1])
                ins.then_inc(ex_done, 1)
                act.wait_ge(ex_done, v + 1)
                step(nc.scalar.activation(lnL[:, b:b + 2], L_[:, b:b + 2], ACT.Ln))
                nc.scalar.activation(rL[:, b:b + 2], lnL[:, b:b + 2], ACT.Exp, scale=-1.0).then_inc(s_inv, 1)

            split_hi(0)
            for t, tk in enumerate(ticks):
                s = tk["seg"]
                if s is not None and segs[s]["first"]:
                    split_hi(segs[s]["chunk"] + 1)
                if t >= 1 and t - 1 < NSEG and t - 1 in norm_no:
                    m = norm_no[t - 1]
                    sg = segs[t - 1]
                    xw = sg["place"][0] in ("memk", "xq")
                    act.wait_ge(ss_done, m + 1)
                    buf = sq[m % 2][:, 0:sg["nt"]]
                    nc.scalar.activation(buf, misc[:, 0:sg["nt"]], ACT.Ln,
                                         bias=(eps_x if xw else eps_a)[:, 0:1]).then_inc(lnexp, 1)
                    act.wait_ge(lnexp, 2 * m + 1)
                    nc.scalar.activation(buf, buf, ACT.Exp, scale=-0.5).then_inc(lnexp, 1)
                for what, v in tk["amid"]:
                    if what == "scores":
                        exps(v)
                    elif what == "values":
                        o_copy(v)
                if s is not None and s in norm_no:
                    sg = segs[s]
                    act.wait_ge(seg_done, s + 1)
                    if norm_no[s] >= 2:
                        act.wait_ge(seg_free, norm_segs[norm_no[s] - 2] + 1)
                    nc.scalar.activation(sq[norm_no[s] % 2][:, 0:sg["nt"]], bank[s % 3][:, 0:sg["nt"]],
                                         ACT.Square).then_inc(sq_ready, 1)
                for what, v in tk["after"]:
                    if what == "scores":
                        exps(v)
                    elif what == "values":
                        o_copy(v)
                for pr, stage in tk["combine"]:
                    if stage == 0:
                        for g in range(3):
                            act.wait_ge(c_dsub, 3 * pr + g + 1)
                            nc.scalar.activation(LS[:, g, :], LS[:, g, :], ACT.Exp).then_inc(c_exp, 1)
                    elif stage == 1:
                        act.wait_ge(c_sum, pr + 1)
                        step(nc.scalar.activation(vsum[:], vsum[:], ACT.Ln))
                        nc.scalar.activation(vsum[:], vsum[:], ACT.Exp, scale=-1.0).then_inc(c_inv, 1)

        @block.gpsimd
        def _(pool):
            for v in range(n_units):
                un = unit(v)
                b = 2 * (v % 3)
                pool.wait_ge(s_inv, v + 1)
                if un["att"]:
                    if v >= 3:
                        pool.wait_ge(ls_done, v - 2)
                    nc.gpsimd.tensor_tensor(lse[:, b:b + 2], lnL[:, b:b + 2], nmax[:, b:b + 2],
                                            ALU.subtract).then_inc(s_lse, 1)
                pm = Pm[v % 3][:, :, 0:un["nk"]]
                nc.gpsimd.tensor_tensor(pm, pm, rL[:, b:b + 2].unsqueeze(2).to_broadcast([P, 2, un["nk"]]),
                                        ALU.mult).then_inc(p_norm, 1)

        @block.vector
        def _(dve):
            steps = [0]

            def step(ins):
                steps[0] += 1
                ins.then_inc(d_chain, 1)
                dve.wait_ge(d_chain, steps[0])

            def split_lo(c):
                dve.wait_ge(hi_ready, c + 1)
                nc.vector.tensor_tensor(wlo[c % NSPL][:], raw[c % NRAW][:], whi[c % NSPL][:].bitcast(F32),
                                        ALU.subtract).then_inc(lo_ready, 1)

            def v_copy(n):
                (kind, m), tl = round_list[n]
                dve.wait_ge(s_vtr, n + 1)
                src = tbank[:].rearrange("p (a b) -> p a b", a=4)
                if kind == "memv":
                    nc.vector.tensor_copy(Vx_early[:, :, m * P:(m + 1) * P], src).then_inc(s_vcp, 1)
                    return
                if m >= 2 and tl[0][0] == 0:
                    dve.wait_ge(pv_done, 10 * (m - 1))
                if m == 1:
                    dve.wait_ge(s_memout, 32)
                for a, (i, _, _, ln) in enumerate(tl):
                    ins = nc.vector.tensor_copy(V[m % 2][0:ln, i, :], src[0:ln, a, :])
                ins.then_inc(s_vcp, 1)

            def finish(s):
                sg = segs[s]
                kind, n = sg["place"]
                src = bank[s % 3][:, 0:sg["nt"]]
                cols = slice(sg["t0"], sg["t0"] + sg["nt"])
                if kind in ("memv", "v"):
                    dve.wait_ge(seg_done, s + 1)
                    if sg["t0"] == 0 and len(done_rounds(s)) > 0:
                        dve.wait_ge(s_vtr, len(done_rounds(s)))
                    nc.vector.tensor_copy(vT[:, cols], src).then_inc(seg_free, 1)
                    return
                m = norm_no[s]
                if kind == "memk":
                    dst, g = Kx_early[:, n, :], gxkc
                elif kind == "q":
                    dst, g = qT[n % 2][:, cols], gqc
                elif kind == "k":
                    dst, g = kT[n % 2][:, cols], gkc
                else:
                    dst, g = xq[n][:, cols], gxqc
                if kind in ("q", "k") and n >= 1 and sg["t0"] == 0:
                    if n == 1 or (n == 0 and kind == "k"):
                        dve.wait_ge(s_memout, 32)
                    if n >= 2:
                        dve.wait_ge(sc_done, 10 * (n - 1))
                if kind in ("q", "k") and n == 0 and sg["t0"] == 0:
                    dve.wait_ge(s_memout, 32)
                if kind == "xq" and sg["t0"] == 0:
                    dve.wait_ge((sc_done, s_vtr, sc_done, pv_done)[n], (50, len(round_list), 60, 60)[n])
                dve.wait_ge(lnexp, 2 * m + 2)
                nc.vector.scalar_tensor_tensor(dst, src, g[:, 0:1], sq[m % 2][:, 0:sg["nt"]], ALU.mult,
                                               ALU.mult).then_inc(seg_free, 1)

            def done_rounds(s):
                return [1 for (pl, _) in round_list if order[pl] < s]

            def biased_max(v):
                un = unit(v)
                b, pm, nk = 2 * (v % 3), Pm[v % 3], un["nk"]
                dve.wait_ge(sc_done, v + 1)
                if v >= 3:
                    dve.wait_ge(tp_done, v - 2)
                    dve.wait_ge(p_norm, v - 2)
                if un["att"]:
                    table = {"window": dist_win, "par2": dist_par2, "par8": dist_par8}[un["bias"]]
                    for h in range(2):
                        sl = -slope(4 * un["g"] + 2 * un["pair"] + h) * DILATION[un["g"]]
                        ins = nc.vector.scalar_tensor_tensor(
                            pm[:, h, 0:nk], table[:, un["boff"]:un["boff"] + nk], sl, s_bank[h][:, 0:nk],
                            ALU.mult, ALU.add)
                    step(ins)
                    src = pm[:, :, 0:nk]
                else:
                    src = pair_bank[:, :, 0:nk]
                nc.vector.tensor_reduce(nmax[:, b:b + 2], src, AX.X, ALU.max, negate=True).then_inc(mx_done, 1)

            def pt_copy(v):
                un = unit(v)
                dve.wait_ge(tp_done, v + 1)
                if v >= 2:
                    dve.wait_ge(pv_done, v - 1)
                src = tbank[:].rearrange("p (h c q) -> p h c q", h=2, c=2)
                dst = PT[v % 2][:].rearrange("p (h c) q -> p h c q", h=2)
                lens = [k[3] for k in un["keys"]] if un["att"] else [P, P]
                if lens == [P, P]:
                    ins = nc.vector.tensor_copy(PT[v % 2][:].rearrange("p a q -> p (a q)"), tbank[:])
                else:
                    for c, ln in enumerate(lens):
                        ins = nc.vector.tensor_copy(dst[0:ln, :, c, :], src[0:ln, :, c, :])
                ins.then_inc(pt_done, 1)

            def lse_copy(v):
                un = unit(v)
                dve.wait_ge(ls_done, v + 1)
                if units[v][1] == 3 and units[v][2] == 0:
                    dve.wait_ge(c_bc, 9)
                nc.vector.tensor_copy(LS[:, un["g"], tok(None, un["base"], un["st"])],
                                      obank[0:2, 256:256 + P]).then_inc(ls_copied, 1)

            def combine(pr, stage):
                last = 30 * (pr + 1)
                if stage == 0:
                    dve.wait_ge(ls_copied, last)
                    step(nc.vector.tensor_tensor(vsum[:], LS[:, 0, :], LS[:, 1, :], ALU.max))
                    step(nc.vector.tensor_tensor(vsum[:], vsum[:], LS[:, 2, :], ALU.max))
                    for g in range(3):
                        nc.vector.tensor_tensor(LS[:, g, :], LS[:, g, :], vsum[:], ALU.subtract).then_inc(c_dsub, 1)
                elif stage == 1:
                    dve.wait_ge(c_exp, 3 * pr + 3)
                    step(nc.vector.tensor_tensor(vsum[:], LS[:, 0, :], LS[:, 1, :], ALU.add))
                    nc.vector.tensor_tensor(vsum[:], vsum[:], LS[:, 2, :], ALU.add).then_inc(c_sum, 1)
                elif stage == 2:
                    dve.wait_ge(c_inv, pr + 1)
                    for g in range(3):
                        ins = nc.vector.tensor_tensor(LS[:, g, :], LS[:, g, :], vsum[:], ALU.mult)
                    ins.then_inc(c_w, 1)
                else:
                    dve.wait_ge(o_copied, last)
                    for n, (t0, nt) in enumerate(SEGS):
                        for g in range(3):
                            dve.wait_ge(c_bc, 9 * pr + 3 * n + g + 1)
                            ot = OT[:, g, t0:t0 + nt]
                            nc.vector.tensor_tensor(ot, ot, w_bank[g][:, 0:nt], ALU.mult).then_inc(c_bu, 1)
                        dve.wait_ge(c_bu, 9 * pr + 3 * n + 3)
                        step(nc.vector.tensor_tensor(oB[:, pr, t0:t0 + nt], OT[:, 0, t0:t0 + nt],
                                                     OT[:, 1, t0:t0 + nt], ALU.add))
                        ins = nc.vector.tensor_tensor(oB[:, pr, t0:t0 + nt], oB[:, pr, t0:t0 + nt],
                                                      OT[:, 2, t0:t0 + nt], ALU.add)
                    ins.then_inc(c_done, 1)

            def units_steps(acts):
                for what, v in acts:
                    if what == "scores":
                        biased_max(v)
                    elif what == "lse":
                        lse_copy(v)
                    elif what == "transposes":
                        pt_copy(v)

            split_lo(0)
            rounds_done = [0]
            for t, tk in enumerate(ticks):
                s = tk["seg"]
                if s is not None and segs[s]["first"]:
                    split_lo(segs[s]["chunk"] + 1)
                units_steps(tk["amid"])
                if t >= 1 and t - 1 < NSEG:
                    finish(t - 1)
                for _ in tk["rounds"]:
                    v_copy(rounds_done[0])
                    rounds_done[0] += 1
                units_steps(tk["after"])
                for pr, stage in tk["combine"]:
                    combine(pr, stage)

        @block.tensor
        def _(pe):
            def product(s, ks):
                sg = segs[s]
                c = sg["chunk"]
                if sg["first"] and 0 in ks:
                    pe.wait_ge(lo_ready, c + 1)
                if s >= 3 and 0 in ks:
                    pe.wait_ge(seg_free, s - 2)
                hi, lo = (memT_hi, memT_lo) if sg["mem"] else (hT_hi, hT_lo)
                cols = slice(sg["t0"], sg["t0"] + sg["nt"])
                out = bank[s % 3][:, 0:sg["nt"]]
                for k in ks:
                    wh, wl = whi[c % NSPL][:, k, :], wlo[c % NSPL][:, k, :]
                    nc.tensor.matmul(out, wh, hi[:, k, cols], start=(k == 0), stop=False)
                    nc.tensor.matmul(out, wh, lo[:, k, cols], start=False, stop=False)
                    ins = nc.tensor.matmul(out, wl, hi[:, k, cols], start=False, stop=(k == KD - 1))
                if KD - 1 in ks:
                    ins.then_inc(seg_done, 1)

            def square_sums(s):
                m = norm_no[s]
                sg = segs[s]
                pe.wait_ge(sq_ready, m + 1)
                if m >= 1:
                    pe.wait_ge(lnexp, 2 * m - 1)
                if bc_before(s):
                    pe.wait_ge(c_bu, bc_before(s))
                w = ones if sg["place"][0] in ("memk", "xq") else pair_ones
                nc.tensor.matmul(misc[:, 0:sg["nt"]], w[:], sq[m % 2][:, 0:sg["nt"]], start=True,
                                 stop=True).then_inc(ss_done, 1)

            def bc_before(s):
                return 9 * sum(1 for tk in ticks[:s + 1] for _, stage in tk["combine"] if stage == 3)

            def v_round(n):
                (kind, m), tl = round_list[n]
                pe.wait_ge(seg_free, order[(kind, m)] + 1)
                free_tbank(("v", n))
                for a, (i, base, st, ln) in enumerate(tl):
                    ins = nc.tensor.transpose(tbank[0:ln, a * P:(a + 1) * P], vT[:, tok(None, base, st, ln)],
                                              ident[:])
                ins.then_inc(s_vtr, 1)

            def free_tbank(use):
                n = use_no[use]
                if n >= 1:
                    kind, i = t_use[n - 1]
                    pe.wait_ge(s_vcp if kind == "v" else pt_done, i + 1)

            def scores(v):
                un = unit(v)
                if v >= 1:
                    pe.wait_ge(mx_done if units[v - 1][0] == "att" else ex_done, v)
                if broadcast[0]:
                    pe.wait_ge(c_bu, broadcast[0])
                if un["att"]:
                    if units[v][2] == 0:
                        pe.wait_ge(seg_free, order[("k", un["ph"])] + 1)
                    q, k = qT[un["buf"]], kT[un["buf"]]
                    k0 = un["keys"][0][1]
                    for h in range(2):
                        r = slice(64 * h, 64 * h + 64)
                        ins = nc.tensor.matmul(s_bank[h][:, 0:un["nk"]], q[r, tok(None, un["base"], un["st"])],
                                               k[r, tok(None, k0, un["st"], un["nk"])], start=True, stop=True)
                else:
                    if units[v][2] == 0:
                        pe.wait_ge(seg_free, order[("xq", un["j"])] + 1)
                    pe.wait_ge(s_memin, 32)
                    for h in range(2):
                        t = 2 * un["t"] + h
                        m0 = 0 if t < 2 else 256
                        ins = nc.tensor.matmul(s_bank[h][:, 0:256], xq[un["j"]][:, t * P:(t + 1) * P],
                                               Kx[:, un["j"], m0:m0 + 256], start=True, stop=True)
                ins.then_inc(sc_done, 1)

            def lse_rows(v):
                b = 2 * (v % 3)
                pe.wait_ge(s_lse, v + 1)
                if values_issued[0]:
                    pe.wait_ge(o_copied, values_issued[0])
                if v >= 1:
                    pe.wait_ge(ls_copied, v)
                nc.tensor.transpose(obank[0:2, 256:256 + P], lse[:, b:b + 2], ident[:]).then_inc(ls_done, 1)

            def transposes(v):
                un = unit(v)
                pe.wait_ge(p_norm, v + 1)
                free_tbank(("u", v))
                lens = [k[3] for k in un["keys"]] if un["att"] else [P, P]
                for h in range(2):
                    c0 = 0
                    for c, ln in enumerate(lens):
                        ins = nc.tensor.transpose(tbank[0:ln, (2 * h + c) * P:(2 * h + c + 1) * P],
                                                  Pm[v % 3][:, h, c0:c0 + ln], ident[:])
                        c0 += ln
                ins.then_inc(tp_done, 1)

            def pv(v):
                un = unit(v)
                pe.wait_ge(pt_done, v + 1)
                if v >= 1:
                    pe.wait_ge(o_copied, v)
                if v < N_ATT:
                    pe.wait_ge(ls_copied, min(v + 2, N_ATT) if lse_issued[0] > v + 1 else v + 1)
                if un["att"] and units[v][2] == 0:
                    wait_rounds_done(pe, ("v", un["ph"]))
                for h in range(2):
                    if un["att"]:
                        for c, (i, _, _, ln) in enumerate(un["keys"]):
                            ins = nc.tensor.matmul(obank[64 * h:64 * h + 64, 0:P],
                                                   V[un["buf"]][0:ln, i, 64 * h:64 * h + 64],
                                                   PT[v % 2][0:ln, 2 * h + c, :], start=(c == 0),
                                                   stop=(c == len(un["keys"]) - 1))
                    else:
                        t = 2 * un["t"] + h
                        m0 = 0 if t < 2 else 2
                        for c in range(2):
                            ins = nc.tensor.matmul(obank[:, h * P:(h + 1) * P],
                                                   Vx[:, m0 + c, un["j"] * P:(un["j"] + 1) * P],
                                                   PT[v % 2][:, 2 * h + c, :], start=(c == 0), stop=(c == 1))
                ins.then_inc(pv_done, 1)
                values_issued[0] += 1

            def broadcasts(pr, t):
                pe.wait_ge(c_w, pr + 1)
                ns = [s for s in norm_segs if s < t]
                pe.wait_ge(lnexp, 2 * len(ns) - 1)
                pe.wait_ge(mx_done, sum(1 for tk in ticks[:t + 1] for w, _ in tk["amid"] + tk["after"]
                                        if w == "scores"))
                for n, (t0, nt) in enumerate(SEGS):
                    for g in range(3):
                        i = 9 * pr + 3 * n + g
                        if i >= 3:
                            pe.wait_ge(c_bu, i - 2)
                        nc.tensor.matmul(w_bank[g][:, 0:nt], head_rows[:], LS[:, g, t0:t0 + nt], start=True,
                                         stop=True).then_inc(c_bc, 1)
                broadcast[0] = 9 * (pr + 1)

            rounds_done = [0]
            lse_issued = [0]
            broadcast = [0]
            values_issued = [0]

            def units_steps(acts):
                for what, v in acts:
                    lse_issued[0] += what == "lse"
                    {"lse": lse_rows, "scores": scores, "transposes": transposes, "values": pv}[what](v)

            for t, tk in enumerate(ticks):
                if tk["seg"] is not None:
                    product(tk["seg"], range(3))
                if t >= 1 and t - 1 in norm_no:
                    square_sums(t - 1)
                units_steps(tk["amid"])
                if tk["seg"] is not None:
                    product(tk["seg"], range(3, KD))
                for _ in tk["rounds"]:
                    v_round(rounds_done[0])
                    rounds_done[0] += 1
                units_steps(tk["after"])
                for pr, stage in tk["combine"]:
                    if stage == 3:
                        broadcasts(pr, t)
    oA = at("oA", [P, NCC, NT], F32, W + 20480)
    ccs = at("ccs", [P, NT], F32, W + 51200)
    NU = NT + 4
    u = at("u", [P, NU], F32, W + 56320)
    cv = at("cv", [P, NT], F32, W + 61472)
    U0 = (1, NP_ + 3, NP_ + 3 + 512)
    S_CONV = NSEG
    cv_step = sem("conv_step")
    sp_passed = sem("passed_by_sync")
    pool_passed = sem("passed_by_pool")
    dve_passed = sem("passed_by_vector")
    CV_STEPS = 3

    def wait(eng, semaphore, value):
        if not (isinstance(value, int) and value <= 0):
            eng.wait_ge(semaphore, value)

    def wait_apart(eng, semaphore, value, passed):
        wait(eng, semaphore, value)
        eng.sem_inc(passed, 1)

    def split_lo(dve, j, c):
        dve.wait_ge(hi_ready, c + 1)
        nc.vector.tensor_tensor(wlo[j % NSPL][:], raw[j % NRAW][:], whi[j % NSPL][:].bitcast(F32),
                                ALU.subtract).then_inc(lo_ready, 1)

    assert C_CONV % 6 == 0 and C_GATE % 6 == 0

    with nc.Block() as block:
        @block.sync
        def _(sp):
            def load_after(i, j):
                wait_apart(sp, lo_ready, C_CONV + 6 * i + j + 1, sp_passed)
                n = j + NRAW
                src = conv_src(2 * i + n // 3, n % 3) if n < 6 or not (isinstance(i, int) and i == 2) else \
                    gate_src(0, n - 6)
                sp.dma_start(raw[j % NRAW][:], src).then_inc(raw_loaded[j % NRAW], 16)

            with sp.Fori(0, 2) as i:
                for j in range(6):
                    load_after(i, j)
            for j in range(6):
                load_after(2, j)

        @block.scalar
        def _(act):
            with act.Fori(0, 3) as i:
                for j in range(6):
                    act.wait_ge(seg_done, S_CONV + 18 * i + 3 * j)
                    jn = j + 1
                    act.wait_ge(raw_loaded[jn % NRAW], 16 * (C_CONV // NRAW + 2 * i + jn // NRAW + 1))
                    nc.scalar.activation(whi[jn % NSPL][:], raw[jn % NRAW][:], ACT.Copy).then_inc(hi_ready, 1)

        @block.vector
        def _(dve):
            for a in (0, NP_ + 1, NU - 1):
                n = 2 if a == NP_ + 1 else 1
                nc.vector.memset(u[:, a:a + n], 0.0).then_inc(d_chain, 1)
            with dve.Fori(0, 3) as i:
                for j in range(6):
                    ch, part, seg0 = 2 * i + j // 3, j % 3, S_CONV + 18 * i + 3 * j
                    split_lo(dve, j + 1, C_CONV + 6 * i + j + 1)
                    for n, (t0, nt) in enumerate(SEGS):
                        dve.wait_ge(seg_done, seg0 + n + 1)
                        src = bank[(S_CONV + n) % 3][:, 0:nt]
                        if part == 0:
                            dve.wait_ge(seg_free, seg0 + n)
                            nc.vector.tensor_copy(ccs[:, t0:t0 + nt], src).then_inc(seg_free, 1)
                        elif part == 1:
                            dve.wait_ge(seg_free, seg0 - 3 + n + 1)
                            nc.vector.tensor_tensor(u[:, U0[n]:U0[n] + nt], src, ccs[:, t0:t0 + nt],
                                                    ALU.mult).then_inc(seg_free, 1)
                        else:
                            if n == 0:
                                dve.wait_ge(seg_free, seg0)
                                step0 = (2 * i + j // 3) * CV_STEPS
                                for tap in range(3):
                                    w = cwc[:, bass.ds(tap * NCC + ch, 1)]
                                    for a, b0, ln in ((0, 1, NP_), (NP_, NP_ + 3, NS_)):
                                        src_u = u[:, b0 + tap - 1:b0 + tap - 1 + ln]
                                        if tap == 0:
                                            ins = nc.vector.tensor_scalar(cv[:, a:a + ln], src_u, w, None, ALU.mult)
                                        else:
                                            ins = nc.vector.scalar_tensor_tensor(cv[:, a:a + ln], src_u, w,
                                                                                 cv[:, a:a + ln], ALU.mult, ALU.add)
                                    ins.then_inc(cv_step, 1)
                                    dve.wait_ge(cv_step, step0 + tap + 1)
                            nc.vector.tensor_tensor(oA[:, bass.ds(ch, 1), t0:t0 + nt].rearrange("p a t -> p (a t)"),
                                                    src, cv[:, t0:t0 + nt], ALU.mult).then_inc(seg_free, 1)

        @block.tensor
        def _(pe):
            with pe.Fori(0, 3) as i:
                for j in range(6):
                    pe.wait_ge(lo_ready, C_CONV + 6 * i + j + 1)
                    for n, (t0, nt) in enumerate(SEGS):
                        seg = S_CONV + 18 * i + 3 * j + n
                        pe.wait_ge(seg_free, seg - 2)
                        out = bank[(S_CONV + n) % 3][:, 0:nt]
                        for k in range(KD):
                            wh, wl = whi[j % NSPL][:, k, :], wlo[j % NSPL][:, k, :]
                            nc.tensor.matmul(out, wh, hT_hi[:, k, t0:t0 + nt], start=(k == 0), stop=False)
                            nc.tensor.matmul(out, wh, hT_lo[:, k, t0:t0 + nt], start=False, stop=False)
                            ins = nc.tensor.matmul(out, wl, hT_hi[:, k, t0:t0 + nt], start=False,
                                                   stop=(k == KD - 1))
                        ins.then_inc(seg_done, 1)

    wbr = [at(f"wbr{i}", [P, 12, P], F32, W + 51200 + 6144 * i) for i in range(2)]
    sig = at("sig", [P, NT], F32, W + 63488)
    acc = [at(f"acc{i}", [P, NT], F32, W + 68608 + 5120 * i) for i in range(2)]
    tmp = at("tmp", [P, NT], F32, W + 78848)
    BR = ((0, NCC, w_bc), (NCC, 2, w_ba), (NCC + 2, XH, w_bx))
    S_GATE = S_CONV + 9 * NCC
    wbr_loaded = [sem(f"wbr_loaded{i}") for i in range(2)]
    g_free = sem("gate_read")
    y_done = sem("branch_done")
    y_free = sem("branch_read")
    acc_step = sem("acc_step")
    m_saved = [sem(f"merged_saved{i}") for i in range(2)]
    gate_done = sem("gate_done")

    with nc.Block() as block:
        @block.sync
        def _(sp):
            def load_wbr(m, h):
                for (k0, nk, w) in BR:
                    sp.dma_start(wbr[h][:, k0:k0 + nk, :], cols_of(w, P * m)).then_inc(wbr_loaded[h], 16)

            def body(i, last):
                for h in range(2):
                    m = 2 * i + h
                    if not (isinstance(i, int) and i == 0):
                        wait_apart(sp, y_done, 9 * m - 9, sp_passed)
                        load_wbr(m, h)
                    for b in range(3):
                        j = 3 * h + b
                        if not (last and h == 1):
                            sp.wait_ge(lo_ready, C_GATE + 6 * i + j + 1)
                            n = j + NRAW
                            sp.dma_start(raw[j % NRAW][:], gate_src(2 * i + n // 3, n % 3)).then_inc(
                                raw_loaded[j % NRAW], 16)
                    sp.wait_ge(acc_step, 2 * m + 2)
                    sp.dma_start(scratch_m[bass.ds(m, 1)].rearrange("a p t -> p (a t)"),
                                 acc[h][:]).then_inc(m_saved[h], 16)

            for h in range(2):
                load_wbr(h, h)
            body(0, False)
            with sp.Fori(1, 3) as i:
                body(i, False)
            body(3, True)
            for h in range(2):
                sp.wait_ge(m_saved[h], 16 * 4)

        @block.scalar
        def _(act):
            def body(i, last):
                for j in range(6):
                    jn = j + 1
                    if not (last and j == 5):
                        wait(act, gate_done, 18 * i + 3 * j)
                        act.wait_ge(raw_loaded[jn % NRAW], 16 * (C_GATE // NRAW + 2 * i + jn // NRAW + 1))
                        nc.scalar.activation(whi[jn % NSPL][:], raw[jn % NRAW][:], ACT.Copy).then_inc(hi_ready, 1)
                    for n, (t0, nt) in enumerate(SEGS):
                        q = 18 * i + 3 * j + n
                        act.wait_ge(gate_done, q + 1)
                        wait(act, y_free, q - 2)
                        nc.scalar.activation(sig[:, t0:t0 + nt], bank[n][:, 0:nt],
                                             ACT.Sigmoid).then_inc(g_free, 1)

            body(0, False)
            with act.Fori(1, 3) as i:
                body(i, False)
            body(3, True)

        @block.vector
        def _(dve):
            def body(i, last):
                for j in range(6):
                    h, b = j // 3, j % 3
                    m = 2 * i + h
                    if not (last and j == 5):
                        split_lo(dve, j + 1, C_GATE + 6 * i + j + 1)
                    if b == 0:
                        wait(dve, m_saved[h], 16 * i)
                    else:
                        wait(dve, acc_step, 2 * m + b - 1)
                    for n, (t0, nt) in enumerate(SEGS):
                        q = 18 * i + 3 * j + n
                        dve.wait_ge(g_free, q + 1)
                        dve.wait_ge(y_done, q + 1)
                        ins = nc.vector.tensor_tensor((acc[h] if b == 0 else tmp)[:, t0:t0 + nt],
                                                      bank[3 + n][:, 0:nt], sig[:, t0:t0 + nt], ALU.mult)
                        ins.then_inc(y_free, 1)
                    if b > 0:
                        dve.wait_ge(y_free, 18 * i + 3 * j + 3)
                        nc.vector.tensor_tensor(acc[h][:], acc[h][:], tmp[:], ALU.add).then_inc(acc_step, 1)

            body(0, False)
            with dve.Fori(1, 3) as i:
                body(i, False)
            body(3, True)

        @block.tensor
        def _(pe):
            def body(i):
                for j in range(6):
                    h, b = j // 3, j % 3
                    pe.wait_ge(lo_ready, C_GATE + 6 * i + j + 1)
                    for n, (t0, nt) in enumerate(SEGS):
                        wait(pe, g_free, 18 * i + 3 * j + n - 2)
                        out = bank[n][:, 0:nt]
                        for k in range(KD):
                            wh, wl = whi[j % NSPL][:, k, :], wlo[j % NSPL][:, k, :]
                            nc.tensor.matmul(out, wh, hT_hi[:, k, t0:t0 + nt], start=(k == 0), stop=False)
                            nc.tensor.matmul(out, wh, hT_lo[:, k, t0:t0 + nt], start=False, stop=False)
                            ins = nc.tensor.matmul(out, wl, hT_hi[:, k, t0:t0 + nt], start=False,
                                                   stop=(k == KD - 1))
                        ins.then_inc(gate_done, 1)
                    k0, nk, _ = BR[b]
                    if b == 0:
                        pe.wait_ge(wbr_loaded[h], 48 * i + 48)
                    o_b = (oA, oB, oC)[b]
                    for n, (t0, nt) in enumerate(SEGS):
                        wait(pe, y_free, 18 * i + 3 * j + n - 2)
                        for k in range(nk):
                            ins = nc.tensor.matmul(bank[3 + n][:, 0:nt], wbr[h][:, k0 + k, :],
                                                   o_b[:, k, t0:t0 + nt], start=(k == 0), stop=(k == nk - 1))
                        ins.then_inc(y_done, 1)

            body(0)
            with pe.Fori(1, 4) as i:
                body(i)

    o = HT
    def place(name, shape, dt=F32):
        nonlocal o
        t = at(name, shape, dt, o)
        size = 4
        for n in shape[1:]:
            size *= n
        o += -(-size // 32) * 32
        return t

    affT = place("affT", [NEXP, NT])
    EC = 256
    NER, NES = 6, 6
    eraw = [place(f"eraw{i}", [P, KD, EC]) for i in range(NER)]
    AFTER_RING = o
    wo_hi = place("wo_hi", [P, KD, D], F32R)
    wo_lo = place("wo_lo", [P, KD, D], F32R)
    g2b = place("g2b", [P, D])
    wr = place("wr", [P, KD, NEXP])
    mg = [place(f"mg{i}", [P, KD, P]) for i in range(2)]
    mg_hi = [place(f"mg_hi{i}", [P, KD, P], F32R) for i in range(2)]
    mg_lo = [place(f"mg_lo{i}", [P, KD, P], F32R) for i in range(2)]
    x1 = [place(f"x1{i}", [P, D]) for i in range(2)]
    tn = [place(f"tn{i}", [P, D]) for i in range(2)]
    tT = place("tT", [P, KD, P])
    expo = place("expo", [P, NEXP])
    aff = place("aff", [P, NEXP])
    st2 = place("st2", [P, 8])
    wo_raw = [place(f"wo_raw{i}", [P, D]) for i in range(2)]
    ENDB4 = o

    wo_loaded = [sem(f"wo_loaded{i}") for i in range(2)]
    wo_h = sem("wo_hi_ready")
    wo_l = sem("wo_lo_ready")
    s_c4 = sem("router_consts")
    mg_loaded = [sem(f"merged_loaded{i}") for i in range(2)]
    mg_h = sem("merged_hi")
    mg_l = sem("merged_lo")
    xr_loaded = [sem(f"residual_loaded{i}") for i in range(2)]
    mm4 = sem("wo_product")
    x1_ready = sem("x1_ready")
    x1_ss = sem("x1_squares")
    x1_rs = sem("x1_rstd")
    t_ready = sem("t_ready")
    t_tr = sem("t_transposed")
    t_cp = sem("tT_copied")
    lg_done = sem("logits")
    lg_max = sem("logits_max")
    lg_exp = sem("logits_exp")
    lg_inv = sem("logits_inverse")
    af_ready = sem("affinities")
    af_tr = sem("affinities_transposed")
    af_cp = sem("affinities_copied")
    x1_saved = [sem(f"x1_saved{i}") for i in range(2)]
    t_saved = [sem(f"t_saved{i}") for i in range(2)]
    er_loaded = [sem(f"expert_raw_loaded{i}") for i in range(NER)]

    mats = [("g", 0), ("u", 0), ("g", 1), ("u", 1), ("g", 2), ("u", 2), ("g", 3), ("u", 3),
            ("d", 0), ("d", 1), ("d", 2), ("d", 3)]
    NCH = len(mats)

    def expert_src(e, j):
        what, c = mats[j]
        w = {"g": w_eg, "u": w_eu, "d": w_ed}[what]
        return w[bass.ds(e, 1), :, c * EC:(c + 1) * EC].rearrange("a (k p) n -> p (a k) n", p=P)

    N4 = NT // P

    def stages(eng, body):
        def peeled(n):
            body(n, n % 2, n // 2, n < N4, 1 <= n <= N4, 2 <= n <= N4 + 1, n >= 3)

        for n in range(4):
            peeled(n)
        with eng.Fori(2, N4 // 2 - 1) as i:
            for h in range(2):
                body(2 * i + h, h, i, True, True, True, True)
        for n in range(N4 - 2, N4 + 3):
            peeled(n)

    def split_next(n):
        return not isinstance(n, int) or 1 <= n < N4 - 1

    with nc.Block() as block:
        @block.sync
        def _(sp):
            for k in range(KD):
                if k >= 2:
                    sp.wait_ge(wo_l, k - 1)
                if k == 0:
                    sp.dma_start(wo_raw[0][:], w_o[0:P, :]).then_inc(wo_loaded[0], 16)
                    for n in range(2):
                        sp.dma_start(mg[n][:], scratch_m[:, :, n * P:(n + 1) * P].rearrange(
                            "k p t -> p k t")).then_inc(mg_loaded[n], 16)
                        sp.dma_start(x1[n][:], x[n * P:(n + 1) * P, :]).then_inc(xr_loaded[n], 16)
                else:
                    sp.dma_start(wo_raw[k % 2][:], w_o[k * P:(k + 1) * P, :]).then_inc(wo_loaded[k % 2], 16)
            sp.dma_start(g2b[:], g2.rearrange("(a n) -> a n", a=1).to_broadcast([P, D])).then_inc(s_c4, 16)
            sp.dma_start(wr[:], w_r.rearrange("(k p) n -> p k n", p=P)).then_inc(s_c4, 16)
            for c in range(NER):
                sp.dma_start(eraw[c][:], expert_src(0, c)).then_inc(er_loaded[c], 16)

            def load(n, h, sixteens):
                sp.wait_ge(mg_l, n - 1)
                sp.dma_start(mg[h][:], scratch_m[:, :, bass.ds(P * n, P)].rearrange(
                    "k p t -> p k t")).then_inc(mg_loaded[h], 16)
                wait_apart(sp, t_ready, n - 1, sp_passed)
                sp.wait_ge(x1_saved[h], sixteens)
                sp.dma_start(x1[h][:], x[bass.ds(P * n, P), :]).then_inc(xr_loaded[h], 16)

            with sp.Fori(1, N4 // 2) as i:
                for h in range(2):
                    load(2 * i + h, h, 16 * i)

        @block.gpsimd
        def _(pool):
            with pool.Fori(0, N4 // 2) as i:
                for h in range(2):
                    n = 2 * i + h
                    pool.wait_ge(x1_ready, n + 1)
                    pool.dma_start(y[bass.ds(P * n, P), :], x1[h][:]).then_inc(x1_saved[h], 16)
                    wait_apart(pool, t_ready, n + 1, pool_passed)
                    pool.dma_start(scratch_t[bass.ds(P * n, P), :], tn[h][:]).then_inc(t_saved[h], 16)
            for h in range(2):
                pool.wait_ge(x1_saved[h], 16 * (N4 // 2))
                pool.wait_ge(t_saved[h], 16 * (N4 // 2))

        @block.scalar
        def _(act):
            nc.scalar.preload_act_table_set("natural_log_exp_and_others")
            for n in range(2):
                act.wait_ge(mg_loaded[n], 16)
                nc.scalar.activation(mg_hi[n][:], mg[n][:], ACT.Copy).then_inc(mg_h, 1)
                for k in range(4 * n, 4 * n + 4):
                    act.wait_ge(wo_loaded[k % 2], 16 * (k // 2 + 1))
                    nc.scalar.activation(wo_hi[:, k, :], wo_raw[k % 2][:], ACT.Copy).then_inc(wo_h, 1)

            def body(n, h, i, now, one, two, three):
                if split_next(n):
                    act.wait_ge(mm4, n)
                    act.wait_ge(mg_loaded[1 - h], 16 * (i + 1 + h))
                    nc.scalar.activation(mg_hi[1 - h][:], mg[1 - h][:], ACT.Copy).then_inc(mg_h, 1)
                if now:
                    act.wait_ge(x1_ready, n + 1)
                    wait(act, t_tr, n - 1)
                    wait(act, t_saved[h], 16 * i)
                    nc.scalar.activation(tn[h][:], x1[h][:], ACT.Square,
                                         accum_out=st2[:, h:h + 1]).then_inc(x1_ss, 1)
                    act.wait_ge(x1_ss, n + 1)
                    nc.scalar.activation(st2[:, h:h + 1], st2[:, h:h + 1], ACT.Ln, bias=eps_d[:, 0:1],
                                         scale=1.0 / D).then_inc(x1_rs, 1)
                    act.wait_ge(x1_rs, 2 * n + 1)
                    nc.scalar.activation(st2[:, h:h + 1], st2[:, h:h + 1], ACT.Exp, scale=-0.5).then_inc(x1_rs, 1)
                if one:
                    act.wait_ge(t_tr, n)
                    wait(act, lg_done, n - 1)
                    nc.scalar.activation(tT[:].rearrange("p k t -> p (k t)"),
                                         pair_bank[:].rearrange("p a b -> p (a b)"), ACT.Copy).then_inc(t_cp, 1)
                if two:
                    act.wait_ge(lg_max, n - 1)
                    wait(act, af_ready, n - 2)
                    nc.scalar.activation(expo[:], bank[4][:, 0:NEXP], ACT.Exp, bias=st2[:, 2:3],
                                         accum_out=st2[:, 3:4]).then_inc(lg_exp, 1)

            stages(act, body)

        @block.vector
        def _(dve):
            for n in range(2):
                dve.wait_ge(mg_h, n + 1)
                nc.vector.tensor_tensor(mg_lo[n][:], mg[n][:], mg_hi[n][:].bitcast(F32),
                                        ALU.subtract).then_inc(mg_l, 1)
                for k in range(4 * n, 4 * n + 4):
                    dve.wait_ge(wo_h, k + 1)
                    nc.vector.tensor_tensor(wo_lo[:, k, :], wo_raw[k % 2][:], wo_hi[:, k, :].bitcast(F32),
                                            ALU.subtract).then_inc(wo_l, 1)
            dve.wait_ge(s_c4, 32)

            def body(n, h, i, now, one, two, three):
                if split_next(n):
                    dve.wait_ge(mg_h, n + 2)
                    nc.vector.tensor_tensor(mg_lo[1 - h][:], mg[1 - h][:], mg_hi[1 - h][:].bitcast(F32),
                                            ALU.subtract).then_inc(mg_l, 1)
                if now:
                    dve.wait_ge(mm4, n + 1)
                    dve.wait_ge(xr_loaded[h], 16 * i + 16)
                    for a in range(2):
                        cols = slice(512 * a, 512 * a + 512)
                        ins = nc.vector.tensor_tensor(x1[h][:, cols], bank[2 * h + a][:], x1[h][:, cols], ALU.add)
                    ins.then_inc(x1_ready, 1)
                if two:
                    dve.wait_ge(lg_done, n - 1)
                    wait(dve, lg_exp, n - 2)
                    nc.vector.tensor_reduce(st2[:, 2:3], bank[4][:, 0:NEXP], AX.X, ALU.max,
                                            negate=True).then_inc(lg_max, 1)
                    dve.wait_ge(lg_exp, n - 1)
                    nc.vector.reciprocal(st2[:, 4:5], st2[:, 3:4]).then_inc(lg_inv, 1)
                    dve.wait_ge(lg_inv, n - 1)
                    wait(dve, af_tr, n - 2)
                    nc.vector.tensor_scalar(aff[:], expo[:], st2[:, 4:5], None, ALU.mult).then_inc(af_ready, 1)
                if now:
                    dve.wait_ge(x1_rs, 2 * n + 2)
                    nc.vector.scalar_tensor_tensor(tn[h][:], x1[h][:], st2[:, h:h + 1], g2b[:], ALU.mult,
                                                   ALU.mult).then_inc(t_ready, 1)
                if three:
                    dve.wait_ge(af_tr, n - 2)
                    nc.vector.tensor_copy(affT[:, bass.ds(P * (n - 3), P)], bank[5][0:NEXP, 0:P]).then_inc(af_cp, 1)

            stages(dve, body)

        @block.tensor
        def _(pe):
            def body(n, h, i, now, one, two, three):
                if now:
                    pe.wait_ge(mg_l, n + 1)
                    wait(pe, x1_ready, n - 1)
                    for a in range(2):
                        cols = slice(512 * a, 512 * a + 512)
                        out = bank[2 * h + a][:]
                        for k in range(KD):
                            if isinstance(n, int) and n == 0 and a == 0:
                                pe.wait_ge(wo_l, k + 1)
                            nc.tensor.matmul(out, mg_hi[h][:, k, :], wo_hi[:, k, cols], start=(k == 0), stop=False)
                            nc.tensor.matmul(out, mg_hi[h][:, k, :], wo_lo[:, k, cols], start=False, stop=False)
                            ins = nc.tensor.matmul(out, mg_lo[h][:, k, :], wo_hi[:, k, cols], start=False,
                                                   stop=(k == KD - 1))
                    ins.then_inc(mm4, 1)
                if two:
                    if isinstance(n, int) and n == 2:
                        pe.wait_ge(s_c4, 32)
                    pe.wait_ge(t_cp, n - 1)
                    wait(pe, af_ready, n - 2)
                    for k in range(KD):
                        ins = nc.tensor.matmul(bank[4][:, 0:NEXP], tT[:, k, :], wr[:, k, :], start=(k == 0),
                                               stop=(k == KD - 1))
                    ins.then_inc(lg_done, 1)
                if one:
                    pe.wait_ge(t_ready, n)
                    wait(pe, t_cp, n - 1)
                    for k in range(KD):
                        ins = nc.tensor.transpose(pair_bank[:, k // 4, (k % 4) * P:(k % 4 + 1) * P],
                                                  tn[1 - h][:, k * P:(k + 1) * P], ident[:])
                    ins.then_inc(t_tr, 1)
                if three:
                    pe.wait_ge(af_ready, n - 2)
                    wait(pe, af_cp, n - 3)
                    nc.tensor.transpose(bank[5][0:NEXP, 0:P], aff[:], ident[:]).then_inc(af_tr, 1)

            stages(pe, body)

    o = AFTER_RING
    ehi = [place(f"ehi{i}", [P, KD, EC], F32R) for i in range(NES)]
    elo = [place(f"elo{i}", [P, KD, EC], F32R) for i in range(NES)]
    xp = place("tokens_hi_lo", [P, KD, 2 * CAP], F32R)
    hid = place("hidden_hi_lo", [P, KD, 2 * CAP], F32R)
    HI, LO = slice(0, CAP), slice(CAP, 2 * CAP)
    low = [place(f"low_product{i}", [P, 2, CAP]) for i in range(2)]
    gate_sum = place("gate_sum", [P, 2, CAP])
    up_sum = place("up_sum", [P, 2, CAP])
    sg = place("silu_gate", [P, 2, CAP])
    hidf = place("hidden", [P, 2, CAP])
    yT = place("yT", [P, KD, CAP])
    y_rows = [place("y_rows_s", [P, D]), place("y_rows_p", [CAP_P, D])]
    xg = [place("x_rows_s", [P, D]), place("x_rows_p", [CAP_P, D])]
    CAPS = (CAP_S, CAP_P)
    gates_r = [place("gates_rows_s", [NEXP, CAP_S]), place("gates_rows_p", [NEXP, CAP_P])]
    idx_r = [place("idx_rows_s", [NEXP, CAP_S]), place("idx_rows_p", [NEXP, CAP_P])]
    gates_c = [place("gates_cols_s", [CAP_S, NEXP]), place("gates_cols_p", [CAP_P, NEXP])]
    idx_c = [place("idx_cols_s", [CAP_S, NEXP], U32), place("idx_cols_p", [CAP_P, NEXP], U32)]
    g_cur = [place("gate_s", [CAP_S, 1]), place("gate_p", [CAP_P, 1])]
    iw_cur = [place("idx_scatter_s", [CAP_S, 1], U32), place("idx_scatter_p", [CAP_P, 1], U32)]
    ig_cur = [place("idx_gather_s", [CAP_S, 1], U32), place("idx_gather_p", [CAP_P, 1], U32)]
    top8 = place("top8", [NEXP, 8])
    top8i = place("top8_idx", [NEXP, 8], U32)

    e_hi = sem("expert_hi")
    e_lo_d = sem("expert_lo_by_vector")
    e_lo_p = sem("expert_lo_by_pool")
    tk = sem("topk_step")
    tk_tr = sem("topk_transposed")
    cols_ready = sem("topk_columns")
    ig_ready = sem("gather_index")
    iw_ready = sem("scatter_index")
    gathered = [sem("gathered_s"), sem("gathered_p")]
    scattered = [sem("scattered_s"), sem("scattered_p")]
    x_tr = sem("x_rows_transposed")
    x_hi = sem("x_tokens_hi")
    x_lo = sem("x_tokens_lo")
    mm5 = sem("expert_product")
    silu_ready = sem("silu_ready")
    h_ready = sem("hidden_ready")
    h_hi = sem("hidden_hi")
    h_lo = sem("hidden_lo")
    low_ready = sem("low_product_copied")
    summed = sem("product_summed")
    y_tr = sem("y_rows_transposed")
    y_rdy = sem("y_rows_ready")
    XB = ((0, 3), (3, 6), (6, 8))
    AHEAD = 4
    ROUNDS = ((CAP_P // 8, 0, NP_, 1), (CAP_S // 8, NP_, NS_, 0))

    def wait_lo(eng, e, j):
        if j % 4 == 3:
            eng.wait_ge(e_lo_p, 3 * e + j // 4 + 1)
        else:
            eng.wait_ge(e_lo_d, 9 * e + j - j // 4 + 1)

    def run_experts(eng, body):
        body(0, False, True)
        body(1, True, True)
        with eng.Fori(2, NEXP - 1) as e:
            body(e, True, True)
        body(NEXP - 1, True, False)

    with nc.Block() as block:
        @block.sync
        def _(sp):
            def body(e, _before, after):
                for j in range(NCH if after else NCH - NER):
                    wait_lo(sp, e, j)
                    sp.sem_inc(sp_passed, 1)
                    jn = j + NER
                    sp.dma_start(eraw[j % NER][:], expert_src(e + jn // NCH, jn % NCH)).then_inc(
                        er_loaded[j % NER], 16)

            run_experts(sp, body)

        @block.gpsimd
        def _(pool):
            def gather(e):
                pool.wait_ge(ig_ready, e + 1)
                wait_apart(pool, x_tr, 3 * e, pool_passed)
                for s in range(2):
                    nc.gpsimd.indirect_dma_start(xg[s][:], None, scratch_t[:],
                                                 bass.IndirectOffsetOnAxis(ap=ig_cur[s][:], axis=0)).then_inc(
                        gathered[s], 16)

            def scatter(e):
                pool.wait_ge(iw_ready, e + 1)
                for s in range(2):
                    pool.wait_ge(y_rdy, 2 * e + s + 1)
                    wait_apart(pool, scattered[s], 16 * e, pool_passed)
                    nc.gpsimd.indirect_dma_start(y[:], bass.IndirectOffsetOnAxis(ap=iw_cur[s][:], axis=0),
                                                 y_rows[s][:], None, compute_op=ALU.add).then_inc(
                        scattered[s], 16)

            def body(e, before, after):
                for j in range(NCH):
                    jn = j + AHEAD
                    if jn % 4 == 3 and (after or jn < NCH):
                        pool.wait_ge(e_hi, NCH * e + jn + 1)
                        nc.gpsimd.tensor_tensor(elo[jn % NES][:], eraw[jn % NER][:], ehi[jn % NES][:].bitcast(F32),
                                                ALU.subtract).then_inc(e_lo_p, 1)
                    if j == 0 and before:
                        scatter(e - 1)
                    if j == 3 and after:
                        gather(e + 1)

            pool.wait_ge(e_hi, 4)
            nc.gpsimd.tensor_tensor(elo[3][:], eraw[3][:], ehi[3][:].bitcast(F32), ALU.subtract).then_inc(e_lo_p, 1)
            gather(0)
            run_experts(pool, body)
            scatter(NEXP - 1)
            for s in range(2):
                pool.wait_ge(scattered[s], 16 * NEXP)

        @block.scalar
        def _(act):
            def hi(e, j):
                act.wait_ge(er_loaded[j % NER], 16 * (2 * e + j // NER + 1))
                nc.scalar.activation(ehi[j % NES][:], eraw[j % NER][:], ACT.Copy).then_inc(e_hi, 1)

            def x_split(e, b):
                act.wait_ge(x_tr, 3 * e + b + 1)
                k0, k1 = XB[b]
                src = bank[4 + b % 2][:, 0:(k1 - k0) * CAP].rearrange("p (k t) -> p k t", t=CAP)
                nc.scalar.activation(xp[:, k0:k1, HI], src, ACT.Copy).then_inc(x_hi, 1)

            def hidden_hi(e, q):
                act.wait_ge(h_ready, 4 * e + q + 1)
                nc.scalar.activation(hid[:, 2 * q:2 * q + 2, HI], hidf[:], ACT.Copy).then_inc(h_hi, 1)

            def y_out(e, s):
                act.wait_ge(iw_ready, e + 1)
                act.wait_ge(y_tr, 2 * e + s + 1)
                wait(act, scattered[s], 16 * e)
                n = CAPS[s]
                nc.scalar.activation(y_rows[s][:], pair_bank[0:n].rearrange("p a b -> p (a b)"), ACT.Copy,
                                     scale=g_cur[s][:, 0:1]).then_inc(y_rdy, 1)

            def body(e, before, after):
                for j in range(NCH):
                    c = NCH * e + j
                    if j == 8:
                        hidden_hi(e, 3)
                    if after or j + AHEAD < NCH:
                        wait(act, mm5, c - (NES - AHEAD) + 1)
                        hi(e, j + AHEAD)
                    if j < 8 and j % 2 == 1:
                        q = 4 * e + j // 2
                        act.wait_ge(summed, c)
                        wait(act, h_ready, q)
                        nc.scalar.activation(sg[:], gate_sum[:], ACT.Silu).then_inc(silu_ready, 1)
                    if 2 <= j < 8 and j % 2 == 0:
                        hidden_hi(e, j // 2 - 1)
                    if after and j == 10:
                        x_split(e + 1, 0)
                        x_split(e + 1, 1)
                    if after and j == 11:
                        x_split(e + 1, 2)
                    if before and j in (1, 2):
                        y_out(e - 1, j - 1)
                    act.wait_ge(mm5, c + 1)
                    wait(act, summed, c - 1)
                    nc.scalar.activation(low[j % 2][:], pairs[j % 2][:, :, LO], ACT.Copy).then_inc(low_ready, 1)

            for j in range(AHEAD):
                hi(0, j)
            for b in range(3):
                x_split(0, b)
            run_experts(act, body)
            for s in range(2):
                y_out(NEXP - 1, s)

        @block.vector
        def _(dve):
            def lo(e, j):
                dve.wait_ge(e_hi, NCH * e + j + 1)
                nc.vector.tensor_tensor(elo[j % NES][:], eraw[j % NER][:], ehi[j % NES][:].bitcast(F32),
                                        ALU.subtract).then_inc(e_lo_d, 1)

            def x_split(e, b):
                dve.wait_ge(x_hi, 3 * e + b + 1)
                k0, k1 = XB[b]
                src = bank[4 + b % 2][:, 0:(k1 - k0) * CAP].rearrange("p (k t) -> p k t", t=CAP)
                nc.vector.tensor_tensor(xp[:, k0:k1, LO], src, xp[:, k0:k1, HI].bitcast(F32),
                                        ALU.subtract).then_inc(x_lo, 1)

            def hidden_lo(e, q):
                dve.wait_ge(h_hi, 4 * e + q + 1)
                pair = hid[:, 2 * q:2 * q + 2]
                nc.vector.tensor_tensor(pair[:, :, LO], hidf[:], pair[:, :, HI].bitcast(F32),
                                        ALU.subtract).then_inc(h_lo, 1)

            def column(e):
                return bass.ds(e, 1)

            def gather_index(e):
                for s in range(2):
                    wait(dve, gathered[s], 16 * e)
                    ins = nc.vector.tensor_copy(ig_cur[s][:], idx_c[s][:, column(e)])
                ins.then_inc(ig_ready, 1)

            def scatter_index(e):
                wait(dve, y_rdy, 2 * e)
                for s in range(2):
                    wait(dve, scattered[s], 16 * e)
                    nc.vector.tensor_copy(g_cur[s][:], gates_c[s][:, column(e)])
                    ins = nc.vector.tensor_copy(iw_cur[s][:], idx_c[s][:, column(e)])
                ins.then_inc(iw_ready, 1)

            def body(e, before, after):
                for j in range(NCH):
                    c = NCH * e + j
                    jn = j + AHEAD
                    if j == 8:
                        hidden_lo(e, 3)
                    if jn % 4 != 3 and (after or jn < NCH):
                        lo(e, jn)
                    if 2 <= j < 8 and j % 2 == 0:
                        hidden_lo(e, j // 2 - 1)
                    if j == 0 and before:
                        scatter_index(e - 1)
                    if j == 3 and after:
                        gather_index(e + 1)
                    if after and j == 10:
                        x_split(e + 1, 0)
                        x_split(e + 1, 1)
                    if after and j == 11:
                        x_split(e + 1, 2)
                    dve.wait_ge(low_ready, c + 1)
                    q = 4 * e + j // 2
                    if j >= 8:
                        if j == 8:
                            wait(dve, y_tr, 2 * e)
                        m = 2 * (j - 8)
                        total = yT[:, m:m + 2, :]
                    elif j % 2 == 0:
                        wait(dve, silu_ready, q)
                        total = gate_sum[:]
                    else:
                        wait(dve, h_ready, q)
                        total = up_sum[:]
                    nc.vector.tensor_tensor(total, pairs[j % 2][:, :, HI], low[j % 2][:], ALU.add).then_inc(
                        summed, 1)
                    if j < 8 and j % 2 == 1:
                        dve.wait_ge(summed, c + 1)
                        dve.wait_ge(silu_ready, q + 1)
                        wait(dve, h_lo, q)
                        nc.vector.tensor_tensor(hidf[:], up_sum[:], sg[:], ALU.mult).then_inc(h_ready, 1)

            for j in range(3):
                lo(0, j)
            nc.vector.memset(top8[:], 0.0).then_inc(tk, 1)
            step = 1
            for rounds, t0, nt, s in ROUNDS:
                row = affT[:, t0:t0 + nt]
                with dve.Fori(0, rounds) as r:
                    at_step = step + 3 * r
                    wait_apart(dve, tk, at_step, dve_passed)
                    nc.vector.max(top8[:], row).then_inc(tk, 1)
                    dve.wait_ge(tk, at_step + 1)
                    nc.vector.tensor_copy(gates_r[s][:, bass.ds(8 * r, 8)], top8[:])
                    nc.vector.max_index(top8i[:], top8[:], row).then_inc(tk, 1)
                    dve.wait_ge(tk, at_step + 2)
                    nc.vector.tensor_scalar(idx_r[s][:, bass.ds(8 * r, 8)], top8i[:], float(t0), None, ALU.add)
                    nc.vector.match_replace(row, top8[:], row, -1.0).then_inc(tk, 1)
                step += 3 * rounds
            dve.wait_ge(tk_tr, 1)
            for s in range(2):
                n = CAPS[s]
                nc.vector.tensor_copy(idx_c[s][:], bank[4 + s][0:n, 0:NEXP])
                ins = nc.vector.tensor_copy(gates_c[s][:], bank[4 + s][0:n, NEXP:2 * NEXP])
            ins.then_inc(cols_ready, 1)
            dve.wait_ge(cols_ready, 1)
            gather_index(0)
            for b in range(3):
                x_split(0, b)
            run_experts(dve, body)
            scatter_index(NEXP - 1)

        @block.tensor
        def _(pe):
            def x_rows(e, b):
                if b == 0:
                    for s in range(2):
                        pe.wait_ge(gathered[s], 16 * e + 16)
                    if isinstance(e, int) and e == 0:
                        pe.wait_ge(cols_ready, 1)
                wait(pe, x_lo, 3 * e + (b == 2))
                k0, k1 = XB[b]
                for k in range(k0, k1):
                    at_k = (k - k0) * CAP
                    f = slice(k * P, (k + 1) * P)
                    nc.tensor.transpose(bank[4 + b % 2][:, at_k:at_k + CAP_S], xg[0][:, f], ident[:])
                    ins = nc.tensor.transpose(bank[4 + b % 2][:, at_k + CAP_S:at_k + CAP], xg[1][:, f],
                                              ident[0:CAP_P, 0:CAP_P])
                ins.then_inc(x_tr, 1)

            def y_back(e, s):
                if s == 0:
                    pe.wait_ge(summed, NCH * e + NCH)
                wait(pe, y_rdy, 2 * e + s)
                n = CAPS[s]
                for k in range(KD):
                    ins = nc.tensor.transpose(pair_bank[0:n, k // 4, (k % 4) * P:(k % 4 + 1) * P],
                                              yT[:, k, s * CAP_S:s * CAP_S + n], ident[:])
                ins.then_inc(y_tr, 1)

            def product(e, j, ks):
                moving = xp if j < 8 else hid
                for m in range(2):
                    out = pairs[j % 2][:, m, 0:2 * CAP]
                    for k in ks:
                        cols = slice(m * P, (m + 1) * P)
                        wh, wl = ehi[j % NES][:, k, cols], elo[j % NES][:, k, cols]
                        nc.tensor.matmul(out, wh, moving[:, k, :], start=(k == 0), stop=False)
                        ins = nc.tensor.matmul(out[:, HI], wl, moving[:, k, HI], start=False, stop=(k == KD - 1))
                return ins

            def body(e, before, after):
                for j in range(NCH):
                    wait_lo(pe, e, j)
                    wait(pe, summed, NCH * e + j - 1)
                    if j == 0:
                        pe.wait_ge(x_lo, 3 * e + 3)
                    if j == 8:
                        pe.wait_ge(h_lo, 4 * e + 3)
                        product(e, j, range(6))
                        pe.wait_ge(h_lo, 4 * e + 4)
                        ins = product(e, j, range(6, KD))
                    else:
                        ins = product(e, j, range(KD))
                    ins.then_inc(mm5, 1)
                    if before and j in (0, 1):
                        y_back(e - 1, j)
                    if after and j == 9:
                        x_rows(e + 1, 0)
                        x_rows(e + 1, 1)
                    if after and j == 10:
                        x_rows(e + 1, 2)

            pe.wait_ge(tk, 1 + 3 * (ROUNDS[0][0] + ROUNDS[1][0]))
            for s in range(2):
                n = CAPS[s]
                nc.tensor.transpose(bank[4 + s][0:n, 0:NEXP], idx_r[s][:], ident[0:NEXP, 0:NEXP])
                ins = nc.tensor.transpose(bank[4 + s][0:n, NEXP:2 * NEXP], gates_r[s][:], ident[0:NEXP, 0:NEXP])
            ins.then_inc(tk_tr, 1)
            for b in range(3):
                x_rows(0, b)
            run_experts(pe, body)
            for s in range(2):
                y_back(NEXP - 1, s)

    ctx.close()


def kernel(**inputs):
    import numpy as np
    import concourse.bacc as bacc
    from concourse import mybir
    from concourse.bass_utils import run_bass_kernel_spmd

    a = {name: np.asarray(value) for name, value in inputs.items()}
    data = {
        "x": np.concatenate([a["x_prompt"][0], a["x_sample"][0]]),
        "mem": np.concatenate([a["mem_prompt"][0], a["mem_sample"][0]]),
        "g1": a["norm1_g"][0], "gm": a["mem_norm_g"][0], "gq": a["q_norm_g"][0], "gk": a["k_norm_g"][0],
        "gxq": a["xq_norm_g"][0], "gxk": a["xk_norm_g"][0], "convw": a["conv_w"][0],
        "w_in": a["w_in"][0], "w_mem": a["w_mem_kv"][0], "w_bc": a["w_br_conv"][0],
        "w_ba": a["w_br_attn"][0], "w_bx": a["w_br_xattn"][0], "w_o": a["w_o"][0],
        "g2": a["norm2_g"][0], "w_r": a["w_router"][0], "w_eg": a["w_exp_gate"][0],
        "w_eu": a["w_exp_up"][0], "w_ed": a["w_exp_down"][0],
    }
    nc = bacc.Bacc("TRN2", target_bir_lowering=False, num_devices=1)
    arrays, args = {}, {}
    for name, value in data.items():
        value = np.ascontiguousarray(value)
        arrays[f"in_{name}"] = value
        args[name] = nc.dram_tensor(f"in_{name}", value.shape, mybir.dt.from_np(value.dtype),
                                    kind="ExternalInput").ap()
    y = nc.dram_tensor("out_y", (NT, D), F32, kind="ExternalOutput").ap()
    kernel_body(nc, y=y, **args)
    rows = run_bass_kernel_spmd(nc, [arrays], core_ids=[0]).results[0]["out_y"]
    return rows[None, :NP_], rows[None, NP_:]
```

```python
from contextlib import ExitStack

import concourse.bass as bass
from concourse import mybir

F32 = mybir.dt.float32
F32R = mybir.dt.float32r
I32 = mybir.dt.int32
U32 = mybir.dt.uint32
ALU = mybir.AluOpType
ACT = mybir.ActivationFunctionType
AX = mybir.AxisListType

P = 128
D = 1024
KD = D // P
NP_, NS_ = 256, 1024
NT = NP_ + NS_
NMEM = 512
CW = 768
NCC = CW // P
E_ATT = 64
NH = 12
E_X = 128
XH = 4
NEXP = 16
CAP_P, CAP_S = 2 * NP_ // NEXP, 2 * NS_ // NEXP
CAP = CAP_P + CAP_S
EPS = 1e-6
BIG = 1e30
SEGS = ((0, 256), (256, 512), (768, 512))
COL_Q, COL_K, COL_V = 3 * CW, 3 * CW + NH * E_ATT, 3 * CW + 2 * NH * E_ATT
COL_X = 3 * CW + 3 * NH * E_ATT
COL_G = COL_X + XH * E_X


def tiles_of(group):
    vtiles, tiles = [], []

    def windowed(base, stride, length):
        first = len(vtiles)
        edges = [0] + list(range(64, length, 128)) + [length]
        for a, b in zip(edges, edges[1:]):
            vtiles.append((base + stride * a, stride, b - a))
        for t in range(length // P):
            keys = [first + t, first + t + 1]
            tiles.append((base + stride * P * t, stride, keys, "window", 64 if t == 0 else 0))

    def whole(base, stride, kind):
        vtiles.append((base, stride, P))
        tiles.append((base, stride, [len(vtiles) - 1], kind, 0))

    if group == 0:
        windowed(0, 1, NP_)
        windowed(NP_, 1, NS_)
    elif group == 1:
        for c in range(2):
            whole(c, 2, "par2")
        for c in range(4):
            windowed(NP_ + c, 4, NS_ // 4)
    else:
        for c in range(2):
            whole(c, 2, "par8")
        for c in range(8):
            whole(NP_ + c, 8, "par2")
    return vtiles, tiles


GEO = [tiles_of(g) for g in range(3)]
DILATION = (1, 4, 16)


def slope(head):
    return 2.0 ** (-8.0 * (head + 1) / NH)


def plan():
    chunks, segs = [], []

    def chunk(src, col, kind, place, over):
        c = len(chunks)
        chunks.append((src, col))
        for n, (t0, nt) in enumerate(over):
            segs.append(dict(chunk=c, first=n == 0, last=n == len(over) - 1, kind=kind, place=place,
                             t0=t0, nt=nt, mem=src == "mem"))

    for j in range(XH):
        chunk("mem", j * P, "k", ("memk", j), ((0, NMEM),))
    for j in range(XH):
        chunk("mem", (XH + j) * P, "v", ("memv", j), ((0, NMEM),))
    for ph in range(6):
        pair, g = ph // 3, ph % 3
        off = g * 4 * E_ATT + pair * P
        chunk("in", COL_Q + off, "q", ("q", ph), SEGS)
        chunk("in", COL_K + off, "k", ("k", ph), SEGS)
        chunk("in", COL_V + off, "v", ("v", ph), SEGS)
    for j in range(XH):
        chunk("in", COL_X + j * P, "q", ("xq", j), SEGS)
    return chunks, segs


def units_of():
    units = []
    for ph in range(6):
        for t in range(10):
            units.append(("att", ph, t))
    for j in range(XH):
        for t in range(5):
            units.append(("mem", j, t))
    return units


def kernel_body(nc, x, mem, g1, gm, gq, gk, gxq, gxk, convw, w_in, w_mem, w_bc, w_ba, w_bx, w_o, g2, w_r,
                w_eg, w_eu, w_ed, y):
    ctx = ExitStack()
    BASE = 16512
    LIMIT = 229344

    def at(name, shape, dt, offset):
        size = 4
        for s in shape[1:]:
            size *= s
        assert BASE + offset + size <= LIMIT, (name, BASE + offset + size)
        return nc.alloc_sbuf_tensor_at(name, shape, dt, offset=BASE + offset)

    def sem(name):
        return ctx.enter_context(nc.semaphore(name))

    chunks, segs = plan()
    units = units_of()
    NSEG = len(segs)

    o = 0

    def small(name, n, dt=F32, parts=P):
        nonlocal o
        t = at(name, [parts, n], dt, o)
        o += -(-4 * n // 32) * 32
        return t

    ident = small("ident", P)
    ones = small("ones", P)
    pair_ones = small("pair_ones", P)
    head_rows = small("head_rows", P, parts=2)
    dist_win = small("dist_win", 256)
    dist_par2 = small("dist_par2", P)
    dist_par8 = small("dist_par8", P)
    gqc = small("gqc", 1)
    gkc = small("gkc", 1)
    gxqc = small("gxqc", 1)
    gxkc = small("gxkc", 1)
    cwc = small("cwc", 3 * NCC)
    eps_d = small("eps_d", 1)
    eps_a = small("eps_a", 1)
    eps_x = small("eps_x", 1)
    sumsq = small("sumsq", 16)
    rstd = small("rstd", 16)
    L_ = small("row_sum", 6)
    lnL = small("ln_sum", 6)
    rL = small("inv_sum", 6)
    nmax = small("neg_max", 6)
    lse = small("lse", 6)
    assert o <= 6400, o
    HT = 6400
    hT_hi = at("hT_hi", [P, KD, NT], F32R, HT)
    hT_lo = at("hT_lo", [P, KD, NT], F32R, HT + 40960)
    RING = HT + 81920
    NRAW, NSPL = 3, 2
    raw = [at(f"raw{i}", [P, KD, P], F32, RING + 4096 * i) for i in range(NRAW)]
    whi = [at(f"whi{i}", [P, KD, P], F32R, RING + 12288 + 4096 * i) for i in range(NSPL)]
    wlo = [at(f"wlo{i}", [P, KD, P], F32R, RING + 20480 + 4096 * i) for i in range(NSPL)]
    OB = RING + 28672
    oB = at("oB", [P, 2, NT], F32, OB)
    vsum = at("vsum", [2, NT], F32, OB + 5120)
    W = OB + 10240
    OT = at("OT", [P, 3, NT], F32, W)
    LS = at("LS", [2, 3, NT], F32, W + 15360)
    oC = at("oC", [P, XH, NT], F32, W)
    qT = [at(f"qT{i}", [P, NT], F32, W + 30720 + 5120 * i) for i in range(2)]
    kT = [at(f"kT{i}", [P, NT], F32, W + 40960 + 5120 * i) for i in range(2)]
    V = [at(f"V{i}", [P, 14, P], F32, W + 51200 + 7168 * i) for i in range(2)]
    vT = at("vT", [P, NT], F32, W + 65536)
    sq = [at(f"sq{i}", [P, 512], F32, W + 70656 + 2048 * i) for i in range(2)]
    Pm = [at(f"Pm{i}", [P, 2, 256], F32, W + 74752 + 2048 * i) for i in range(3)]
    PT = [at(f"PT{i}", [P, 4, P], F32, W + 80896 + 2048 * i) for i in range(2)]
    memT_hi = at("memT_hi", [P, KD, NMEM], F32R, W)
    memT_lo = at("memT_lo", [P, KD, NMEM], F32R, W + 16384)
    Kx_early = at("Kx_early", [P, XH, NMEM], F32, W + 32768 + 2048 + 1024)
    Vx_early = at("Vx_early", [P, 4, XH * P], F32, W + 57344)
    Kx = at("Kx", [P, XH, NMEM], F32, W + 40960)
    Vx = at("Vx", [P, 4, XH * P], F32, W + 49152)
    xq = [qT[0], vT, qT[1], at("xq3", [P, NT], F32, W + 57344)]
    scratch_kx = nc.dram_tensor("scratch_kx", [P, XH * NMEM], F32, kind="Internal").ap()
    scratch_vx = nc.dram_tensor("scratch_vx", [P, 4 * XH * P], F32, kind="Internal").ap()
    scratch_m = nc.dram_tensor("scratch_m", [KD, P, NT], F32, kind="Internal").ap()
    scratch_t = nc.dram_tensor("scratch_t", [NT, D], F32, kind="Internal").ap()

    pairs = [ctx.enter_context(nc.psum_tensor(f"bank_pair{i}", [P, 2, 512], F32)) for i in range(4)]
    bank = [pairs[i // 2][:, i % 2, :] for i in range(6)]
    pair_bank = pairs[3]

    s_const = sem("const_loaded")
    s_ident = sem("consts_made")
    s_dist = sem("distances")
    s_dchain = sem("distances_step")
    NXT = 5
    s_xin = [sem(f"x_loaded{i}") for i in range(NXT)]
    s_ss = sem("x_squares")
    s_rs = sem("x_rstd")
    s_xn = sem("x_normed")
    s_tr = sem("x_transposed")
    s_hi = sem("x_hi")
    s_lo = sem("x_lo")
    xt = [at(f"xt{i}", [P, D], F32, W + (32768 if i < 3 else 73728 - 12288) + 4096 * i) for i in range(NXT)]
    xn = [at(f"xn{i}", [P, D], F32, W + 45056 + 4096 * i) for i in range(2)]
    g_rows = [at("g1_rows", [P, D], F32, W + 65536), at("gm_rows", [P, D], F32, W + 69632)]
    s_gain = [sem("x_gain_loaded"), sem("memory_gain_loaded")]
    junk = at("junk", [P, D], F32, W + 57344)
    dwork = at("dwork", [P, 3, 256], F32, W + 61440)
    diwork = at("diwork", [P, 2, 128], I32, W + 64512)

    tile_src = [("x", i) for i in range(NT // P)] + [("m", i) for i in range(NMEM // P)]
    NTILE = len(tile_src)

    raw_loaded = [sem(f"raw_loaded{i}") for i in range(NRAW)]
    hi_ready = sem("whi_ready")
    lo_ready = sem("wlo_ready")

    n_straight = len(chunks)

    C_CONV = n_straight
    C_GATE = C_CONV + 3 * NCC
    C_END = C_GATE + 3 * KD
    CONV_COLS = (CW, 2 * CW, 0)

    def cols_of(w, col):
        return w[:, bass.ds(col, P)].rearrange("(k p) n -> p k n", p=P)

    def conv_src(ch, part):
        return cols_of(w_in, CONV_COLS[part] + P * ch)

    def gate_src(m, b):
        return cols_of(w_in, COL_G + D * b + P * m)

    def chunk_src(c):
        if c >= C_GATE:
            return gate_src((c - C_GATE) // 3, (c - C_GATE) % 3)
        if c >= C_CONV:
            return conv_src((c - C_CONV) // 3, (c - C_CONV) % 3)
        src, col = chunks[c]
        return cols_of(w_mem if src == "mem" else w_in, col)

    with nc.Block() as block:
        @block.sync
        def _(sp):
            ctx.enter_context(nc.allow_non_contiguous_dma(reason="a few vectors"))

            def gain_rows(g, i):
                sp.dma_start(g_rows[i][:], g.rearrange("(a n) -> a n", a=1).to_broadcast([P, D])).then_inc(
                    s_gain[i], 16)

            for n in range(NXT):
                sp.dma_start(xt[n][:], x[n * P:(n + 1) * P, :]).then_inc(s_xin[n], 16)
                if n == 1:
                    gain_rows(g1, 0)
            gain_rows(gm, 1)
            for h in range(2):
                sp.dma_start(gqc[64 * h:64 * h + 64, :], gq.rearrange("(p a) -> p a", a=1)).then_inc(s_const, 16)
                sp.dma_start(gkc[64 * h:64 * h + 64, :], gk.rearrange("(p a) -> p a", a=1)).then_inc(s_const, 16)
            sp.dma_start(gxqc[:], gxq.rearrange("(p a) -> p a", a=1)).then_inc(s_const, 16)
            sp.dma_start(gxkc[:], gxk.rearrange("(p a) -> p a", a=1)).then_inc(s_const, 16)
            sp.dma_start(cwc[:].rearrange("p (j c) -> p j c", j=3),
                         convw.rearrange("j (c p) -> p j c", p=P)).then_inc(s_const, 16)
            for n, (src, i) in enumerate(tile_src):
                if n >= NXT:
                    sp.wait_ge(s_xn, n - NXT + 1)
                    a = (x if src == "x" else mem)[i * P:(i + 1) * P, :]
                    sp.dma_start(xt[n % NXT][:], a).then_inc(s_xin[n % NXT], 16)
            for c in range(NRAW):
                sp.dma_start(raw[c][:], chunk_src(c)).then_inc(raw_loaded[c], 16)

        @block.gpsimd
        def _(pool):
            pool.memset(ident[:], 0.0).then_inc(s_ident, 1)
            pool.memset(ones[:], 1.0)
            pool.memset(head_rows[:], 1.0)
            pool.memset(eps_d[:], EPS)
            pool.memset(eps_a[:], EPS * E_ATT)
            pool.memset(eps_x[:], EPS * E_X).then_inc(s_ident, 1)
            pool.wait_ge(s_ident, 2)
            pool.affine_select(out=ident[:], in_=ident[:], compare_op=ALU.not_equal, fill=1.0, base=0,
                               pattern=[[-1, P]], channel_multiplier=1).then_inc(s_ident, 1)
            pool.affine_select(out=head_rows[:], in_=head_rows[:], compare_op=ALU.is_ge, fill=0.0, base=0,
                               pattern=[[1, P]], channel_multiplier=-64).then_inc(s_ident, 1)
            pool.wait_ge(s_ident, 4)
            pool.affine_select(out=head_rows[:], in_=head_rows[:], compare_op=ALU.is_ge, fill=0.0, base=63,
                               pattern=[[-1, P]], channel_multiplier=64).then_inc(s_ident, 1)
            pool.iota(dwork[:, 0, :], [[1, 256]], base=-64, channel_multiplier=-1,
                      allow_small_or_imprecise_dtypes=True)
            pool.iota(dwork[:, 1, 0:P], [[1, P]], base=0, channel_multiplier=-1,
                      allow_small_or_imprecise_dtypes=True)
            pool.iota(diwork[:, 0, :], [[1, P]], base=0, channel_multiplier=-1).then_inc(s_dist, 1)
            pool.wait_ge(s_dist, 2)
            pool.affine_select(out=dist_win[:], in_=dist_win[:], compare_op=ALU.is_ge, fill=BIG, base=128,
                               pattern=[[-1, 256]], channel_multiplier=1).then_inc(s_dist, 1)
            pool.wait_ge(s_dist, 3)
            pool.affine_select(out=dist_win[:], in_=dist_win[:], compare_op=ALU.is_ge, fill=BIG, base=0,
                               pattern=[[1, 256]], channel_multiplier=-1).then_inc(s_dist, 1)

        @block.scalar
        def _(act):
            nc.scalar.preload_act_table_set("natural_log_exp_and_others")
            act.wait_ge(s_ident, 2)
            for n in range(NTILE + 1):
                if n < NTILE:
                    act.wait_ge(s_xin[n % NXT], 16 * (n // NXT + 1))
                    if n >= 1:
                        act.wait_ge(s_rs, 2 * n)
                    nc.scalar.activation(junk[:], xt[n % NXT][:], ACT.Square,
                                         accum_out=sumsq[:, n:n + 1]).then_inc(s_ss, 1)
                    act.wait_ge(s_ss, n + 1)
                    nc.scalar.activation(rstd[:, n:n + 1], sumsq[:, n:n + 1], ACT.Ln, bias=eps_d[:, 0:1],
                                         scale=1.0 / D).then_inc(s_rs, 1)
                    act.wait_ge(s_rs, 2 * n + 1)
                    nc.scalar.activation(rstd[:, n:n + 1], rstd[:, n:n + 1], ACT.Exp,
                                         scale=-0.5).then_inc(s_rs, 1)
                if n >= 1:
                    m = n - 1
                    act.wait_ge(s_tr, m + 1)
                    dst, i = (hT_hi, m) if m < 10 else (memT_hi, m - 10)
                    nc.scalar.activation(dst[:, :, i * P:(i + 1) * P],
                                         pairs[m % 2][:].rearrange("p a (k t) -> p (a k) t", t=P),
                                         ACT.Copy).then_inc(s_hi, 1)

        @block.vector
        def _(dve):
            steps = [0]

            def step(ins):
                steps[0] += 1
                ins.then_inc(s_dchain, 1)
                dve.wait_ge(s_dchain, steps[0])

            for a in range(2):
                for b in range(2):
                    nc.vector.memset(pair_ones[64 * a:64 * a + 64, 64 * b:64 * b + 64], float(a == b))
            dve.wait_ge(s_dist, 1)
            step(nc.vector.tensor_scalar(dwork[:, 2, :], dwork[:, 0, :], -1.0, None, ALU.mult))
            nc.vector.tensor_tensor(dist_win[:], dwork[:, 0, :], dwork[:, 2, :], ALU.max).then_inc(s_dist, 1)
            dve.wait_ge(s_dist, 2)
            step(nc.vector.tensor_scalar(dwork[:, 2, 0:P], dwork[:, 1, 0:P], -1.0, None, ALU.mult))
            step(nc.vector.tensor_tensor(dwork[:, 0, 0:P], dwork[:, 1, 0:P], dwork[:, 2, 0:P], ALU.max))
            for mask, out in ((1, dist_par2), (7, dist_par8)):
                step(nc.vector.tensor_scalar(diwork[:, 1, :], diwork[:, 0, :], mask, None, ALU.bitwise_and))
                step(nc.vector.tensor_copy(dwork[:, 1, 0:P], diwork[:, 1, :]))
                step(nc.vector.tensor_scalar(dwork[:, 2, 0:P], dwork[:, 1, 0:P], BIG, None, ALU.mult))
                step(nc.vector.scalar_tensor_tensor(out[:], dwork[:, 0, 0:P], 1.0 / (mask + 1), dwork[:, 2, 0:P],
                                                    ALU.mult, ALU.add))
            for n in range(NTILE + 1):
                if n < NTILE:
                    dve.wait_ge(s_rs, 2 * n + 2)
                    if n >= 2:
                        dve.wait_ge(s_xn, n - 1)
                        dve.wait_ge(s_tr, n - 1)
                    if n in (0, NT // P):
                        dve.wait_ge(s_gain[n > 0], 16)
                    nc.vector.scalar_tensor_tensor(xn[n % 2][:], xt[n % NXT][:], rstd[:, n:n + 1],
                                                   g_rows[n >= NT // P][:], ALU.mult, ALU.mult).then_inc(s_xn, 1)
                if n >= 1:
                    m = n - 1
                    dve.wait_ge(s_hi, m + 1)
                    hi, lo, i = (hT_hi, hT_lo, m) if m < 10 else (memT_hi, memT_lo, m - 10)
                    nc.vector.tensor_tensor(lo[:, :, i * P:(i + 1) * P],
                                            pairs[m % 2][:].rearrange("p a (k t) -> p (a k) t", t=P),
                                            hi[:, :, i * P:(i + 1) * P].bitcast(F32),
                                            ALU.subtract).then_inc(s_lo, 1)
            dve.wait_ge(s_const, 16 * 7)
            step(nc.vector.tensor_scalar(gkc[:], gkc[:], float(E_ATT) ** 0.5, None, ALU.mult))
            step(nc.vector.tensor_scalar(gxkc[:], gxkc[:], float(E_X) ** 0.5, None, ALU.mult))

        @block.tensor
        def _(pe):
            pe.wait_ge(s_ident, 3)
            for n in range(NTILE):
                pe.wait_ge(s_xn, n + 1)
                if n >= 2:
                    pe.wait_ge(s_lo, n - 1)
                for k in range(KD):
                    ins = nc.tensor.transpose(pairs[n % 2][:, k // 4, (k % 4) * P:(k % 4 + 1) * P],
                                              xn[n % 2][:, k * P:(k + 1) * P], ident[:])
                ins.then_inc(s_tr, 1)

    seg_done = sem("seg_done")
    seg_free = sem("seg_free")
    sq_ready = sem("sq_ready")
    ss_done = sem("ss_done")
    lnexp = sem("lnexp")
    sc_done = sem("scores_done")
    mx_done = sem("max_done")
    ex_done = sem("exp_done")
    s_inv = sem("inv_sum_ready")
    s_lse = sem("lse_ready")
    p_norm = sem("probs_normed")
    tp_done = sem("probs_transposed")
    pt_done = sem("pt_copied")
    ls_done = sem("lse_transposed")
    ls_copied = sem("lse_copied")
    pv_done = sem("pv_done")
    o_copied = sem("o_copied")
    a_chain = sem("act_step")
    d_chain = sem("dve_step")
    s_memout = sem("mem_kv_saved")
    s_memin = sem("mem_kv_loaded")
    s_vtr = sem("v_transposed")
    s_vcp = sem("v_copied")
    c_dsub = sem("combine_differences")
    c_exp = sem("combine_exps")
    c_sum = sem("combine_sum")
    c_inv = sem("combine_inverse")
    c_w = sem("combine_weights")
    c_bc = sem("weights_broadcast")
    c_bu = sem("broadcast_used")
    c_done = sem("combined")

    s_bank = (pair_bank[:, 0, :], pair_bank[:, 1, :])
    misc, tbank, obank = bank[3], bank[4], bank[5]
    w_bank = (misc, *s_bank)
    norm_segs = [s for s in range(NSEG) if segs[s]["kind"] != "v"]
    norm_no = {s: n for n, s in enumerate(norm_segs)}
    last_seg = {sg["chunk"]: s for s, sg in enumerate(segs)}

    def v_rounds(place):
        kind, n = place
        if kind == "memv":
            return [[(t, P * t, 1, P) for t in range(4)]]
        vt = [(i, a, st, ln) for i, (a, st, ln) in enumerate(GEO[n % 3][0])]
        return [vt[i:i + 4] for i in range(0, len(vt), 4)]

    EXTRA = 14
    MID = 2
    ticks = [dict(seg=s if s < NSEG else None, units=[], rounds=[], combine=[], amid=[], after=[])
             for s in range(NSEG + EXTRA)]
    order = {sg["place"]: s for s, sg in enumerate(segs) if sg["last"]}
    for s, sg in enumerate(segs):
        if sg["kind"] == "v" and sg["last"]:
            for i, r in enumerate(v_rounds(sg["place"])):
                ticks[s + 1 + i // 2]["rounds"].append((sg["place"], r))
    n_units = len(units)
    for ph in range(6):
        start = order[("v", ph)] + 3 + 2 * (ph == 3)
        room = {3: 5, 5: 4}.get(ph, 7)
        for i in range(10):
            ticks[start + i * room // 10]["units"].append(10 * ph + i)
        if ph % 3 == 2:
            for i in range(4):
                ticks[start + room + 1 + i]["combine"].append((ph // 3, i))
            after = start + room + 5
    for i in range(n_units - 60):
        ticks[after + i // 5]["units"].append(60 + i)
    scored, transposed = [], []
    for tk in ticks:
        for n, v in enumerate(tk["units"] or [None]):
            acts = tk["amid" if n == 0 and tk["seg"] is not None else "after"]
            ready = transposed[:]
            transposed.clear()
            if v is not None:
                scored.append(v)
            u = scored.pop(0) if scored and (v is None or len(scored) > 2) else None
            if u is not None and u < 60:
                acts.append(("lse", u))
            if v is not None:
                acts.append(("scores", v))
            if u is not None:
                acts.append(("transposes", u))
                transposed.append(u)
            acts += [("values", w) for w in ready]
    assert not scored and not transposed

    t_use, use_no, round_list = [], {}, []
    for tk in ticks:
        uses = [("u", v) for what, v in tk["amid"] if what == "transposes"]
        for r in tk["rounds"]:
            uses.append(("v", len(round_list)))
            round_list.append(r)
        uses += [("u", v) for what, v in tk["after"] if what == "transposes"]
        for use in uses:
            use_no[use] = len(t_use)
            t_use.append(use)

    att_units = [v for v in range(n_units) if units[v][0] == "att"]
    N_ATT = len(att_units)

    def unit(v):
        kind, n, t = units[v]
        if kind == "att":
            vt, tl = GEO[n % 3]
            base, st, keys, bias, boff = tl[t]
            kk = [(i, *vt[i]) for i in keys]
            return dict(att=True, ph=n, g=n % 3, pair=n // 3, base=base, st=st, keys=kk, bias=bias, boff=boff,
                        nk=sum(k[3] for k in kk), buf=n % 2)
        return dict(att=False, j=n, t=t, buf=n % 2, nk=256)

    def tok(t, base, st, n=P):
        return slice(base, base + st * (n - 1) + 1, st) if st > 1 else slice(base, base + n)

    def wait_rounds_done(eng, place):
        n = max(i for i, (pl, _) in enumerate(round_list) if pl == place)
        eng.wait_ge(s_vcp, n + 1)

    with nc.Block() as block:
        @block.sync
        def _(sp):
            for c in range(NRAW, n_straight + NRAW):
                sp.wait_ge(lo_ready, c - NRAW + 1)
                if c < C_END:
                    sp.dma_start(raw[c % NRAW][:], chunk_src(c)).then_inc(raw_loaded[c % NRAW], 16)
                if c == 11:
                    sp.wait_ge(seg_free, 8)
                    sp.wait_ge(s_vcp, 4)
                    sp.dma_start(scratch_kx, Kx_early[:].rearrange("p a b -> p (a b)")).then_inc(s_memout, 16)
                    sp.dma_start(scratch_vx, Vx_early[:].rearrange("p a b -> p (a b)")).then_inc(s_memout, 16)
            sp.wait_ge(s_memout, 32)
            sp.wait_ge(pv_done, N_ATT)
            sp.dma_start(Kx[:].rearrange("p a b -> p (a b)"), scratch_kx).then_inc(s_memin, 16)
            sp.dma_start(Vx[:].rearrange("p a b -> p (a b)"), scratch_vx).then_inc(s_memin, 16)

        @block.scalar
        def _(act):
            steps = [0]

            def step(ins):
                steps[0] += 1
                ins.then_inc(a_chain, 1)
                act.wait_ge(a_chain, steps[0])

            def split_hi(c):
                act.wait_ge(raw_loaded[c % NRAW], 16 * (c // NRAW + 1))
                if c >= NSPL:
                    act.wait_ge(seg_done, last_seg[c - NSPL] + 1)
                nc.scalar.activation(whi[c % NSPL][:], raw[c % NRAW][:], ACT.Copy).then_inc(hi_ready, 1)

            def o_copy(v):
                un = unit(v)
                act.wait_ge(pv_done, v + 1)
                if un["att"]:
                    dst = OT[:, un["g"], tok(None, un["base"], un["st"])]
                    if un["g"] == 0 and un["pair"] == 1 and units[v][2] == 0:
                        act.wait_ge(c_done, 1)
                    nc.scalar.activation(dst, obank[:, 0:P], ACT.Copy).then_inc(o_copied, 1)
                else:
                    act.wait_ge(c_done, 2)
                    nc.scalar.activation(oC[:, un["j"], 2 * P * un["t"]:2 * P * (un["t"] + 1)],
                                         obank[:, 0:2 * P], ACT.Copy).then_inc(o_copied, 1)

            def exps(v):
                un = unit(v)
                act.wait_ge(mx_done, v + 1)
                pm, nk, b = Pm[v % 3], un["nk"], 2 * (v % 3)
                if v >= 3:
                    act.wait_ge(p_norm, v - 2)
                for h in range(2):
                    src = pm[:, h, 0:nk] if un["att"] else s_bank[h][:, 0:nk]
                    ins = nc.scalar.activation(pm[:, h, 0:nk], src, ACT.Exp, bias=nmax[:, b + h:b + h + 1],
                                               accum_out=L_[:, b + h:b + h + 1])
                ins.then_inc(ex_done, 1)
                act.wait_ge(ex_done, v + 1)
                step(nc.scalar.activation(lnL[:, b:b + 2], L_[:, b:b + 2], ACT.Ln))
                nc.scalar.activation(rL[:, b:b + 2], lnL[:, b:b + 2], ACT.Exp, scale=-1.0).then_inc(s_inv, 1)

            split_hi(0)
            for t, tk in enumerate(ticks):
                s = tk["seg"]
                if t >= 1 and t - 1 < NSEG and t - 1 in norm_no:
                    m = norm_no[t - 1]
                    sg = segs[t - 1]
                    xw = sg["place"][0] in ("memk", "xq")
                    act.wait_ge(ss_done, m + 1)
                    buf = sq[m % 2][:, 0:sg["nt"]]
                    nc.scalar.activation(buf, misc[:, 0:sg["nt"]], ACT.Ln,
                                         bias=(eps_x if xw else eps_a)[:, 0:1]).then_inc(lnexp, 1)
                    act.wait_ge(lnexp, 2 * m + 1)
                    nc.scalar.activation(buf, buf, ACT.Exp, scale=-0.5).then_inc(lnexp, 1)
                for what, v in tk["amid"]:
                    if what == "scores":
                        exps(v)
                    elif what == "values":
                        o_copy(v)
                if s is not None and segs[s]["first"]:
                    split_hi(segs[s]["chunk"] + 1)
                if s is not None and s in norm_no:
                    sg = segs[s]
                    act.wait_ge(seg_done, s + 1)
                    if norm_no[s] >= 2:
                        act.wait_ge(seg_free, norm_segs[norm_no[s] - 2] + 1)
                    nc.scalar.activation(sq[norm_no[s] % 2][:, 0:sg["nt"]], bank[s % 3][:, 0:sg["nt"]],
                                         ACT.Square).then_inc(sq_ready, 1)
                for what, v in tk["after"]:
                    if what == "scores":
                        exps(v)
                    elif what == "values":
                        o_copy(v)
                for pr, stage in tk["combine"]:
                    if stage == 0:
                        for g in range(3):
                            act.wait_ge(c_dsub, 3 * pr + g + 1)
                            nc.scalar.activation(LS[:, g, :], LS[:, g, :], ACT.Exp).then_inc(c_exp, 1)
                    elif stage == 1:
                        act.wait_ge(c_sum, pr + 1)
                        step(nc.scalar.activation(vsum[:], vsum[:], ACT.Ln))
                        nc.scalar.activation(vsum[:], vsum[:], ACT.Exp, scale=-1.0).then_inc(c_inv, 1)

        @block.gpsimd
        def _(pool):
            for v in range(n_units):
                un = unit(v)
                b = 2 * (v % 3)
                pool.wait_ge(s_inv, v + 1)
                if un["att"]:
                    if v >= 3:
                        pool.wait_ge(ls_done, v - 2)
                    nc.gpsimd.tensor_tensor(lse[:, b:b + 2], lnL[:, b:b + 2], nmax[:, b:b + 2],
                                            ALU.subtract).then_inc(s_lse, 1)
                pm = Pm[v % 3][:, :, 0:un["nk"]]
                nc.gpsimd.tensor_tensor(pm, pm, rL[:, b:b + 2].unsqueeze(2).to_broadcast([P, 2, un["nk"]]),
                                        ALU.mult).then_inc(p_norm, 1)

        @block.vector
        def _(dve):
            steps = [0]

            def step(ins):
                steps[0] += 1
                ins.then_inc(d_chain, 1)
                dve.wait_ge(d_chain, steps[0])

            def split_lo(c):
                dve.wait_ge(hi_ready, c + 1)
                nc.vector.tensor_tensor(wlo[c % NSPL][:], raw[c % NRAW][:], whi[c % NSPL][:].bitcast(F32),
                                        ALU.subtract).then_inc(lo_ready, 1)

            def v_copy(n):
                (kind, m), tl = round_list[n]
                dve.wait_ge(s_vtr, n + 1)
                src = tbank[:].rearrange("p (a b) -> p a b", a=4)
                if kind == "memv":
                    nc.vector.tensor_copy(Vx_early[:, :, m * P:(m + 1) * P], src).then_inc(s_vcp, 1)
                    return
                if m >= 2 and tl[0][0] == 0:
                    dve.wait_ge(pv_done, 10 * (m - 1))
                if m == 1:
                    dve.wait_ge(s_memout, 32)
                for a, (i, _, _, ln) in enumerate(tl):
                    ins = nc.vector.tensor_copy(V[m % 2][0:ln, i, :], src[0:ln, a, :])
                ins.then_inc(s_vcp, 1)

            def finish(s):
                sg = segs[s]
                kind, n = sg["place"]
                src = bank[s % 3][:, 0:sg["nt"]]
                cols = slice(sg["t0"], sg["t0"] + sg["nt"])
                if kind in ("memv", "v"):
                    dve.wait_ge(seg_done, s + 1)
                    if sg["t0"] == 0 and len(done_rounds(s)) > 0:
                        dve.wait_ge(s_vtr, len(done_rounds(s)))
                    nc.vector.tensor_copy(vT[:, cols], src).then_inc(seg_free, 1)
                    return
                m = norm_no[s]
                if kind == "memk":
                    dst, g = Kx_early[:, n, :], gxkc
                elif kind == "q":
                    dst, g = qT[n % 2][:, cols], gqc
                elif kind == "k":
                    dst, g = kT[n % 2][:, cols], gkc
                else:
                    dst, g = xq[n][:, cols], gxqc
                if kind in ("q", "k") and n >= 1 and sg["t0"] == 0:
                    if n == 1 or (n == 0 and kind == "k"):
                        dve.wait_ge(s_memout, 32)
                    if n >= 2:
                        dve.wait_ge(sc_done, 10 * (n - 1))
                if kind in ("q", "k") and n == 0 and sg["t0"] == 0:
                    dve.wait_ge(s_memout, 32)
                if kind == "xq" and sg["t0"] == 0:
                    dve.wait_ge((sc_done, s_vtr, sc_done, pv_done)[n], (50, len(round_list), 60, 60)[n])
                dve.wait_ge(lnexp, 2 * m + 2)
                nc.vector.scalar_tensor_tensor(dst, src, g[:, 0:1], sq[m % 2][:, 0:sg["nt"]], ALU.mult,
                                               ALU.mult).then_inc(seg_free, 1)

            def done_rounds(s):
                return [1 for (pl, _) in round_list if order[pl] < s]

            def biased_max(v):
                un = unit(v)
                b, pm, nk = 2 * (v % 3), Pm[v % 3], un["nk"]
                dve.wait_ge(sc_done, v + 1)
                if v >= 3:
                    dve.wait_ge(tp_done, v - 2)
                    dve.wait_ge(p_norm, v - 2)
                if un["att"]:
                    table = {"window": dist_win, "par2": dist_par2, "par8": dist_par8}[un["bias"]]
                    for h in range(2):
                        sl = -slope(4 * un["g"] + 2 * un["pair"] + h) * DILATION[un["g"]]
                        ins = nc.vector.scalar_tensor_tensor(
                            pm[:, h, 0:nk], table[:, un["boff"]:un["boff"] + nk], sl, s_bank[h][:, 0:nk],
                            ALU.mult, ALU.add)
                    step(ins)
                    src = pm[:, :, 0:nk]
                else:
                    src = pair_bank[:, :, 0:nk]
                nc.vector.tensor_reduce(nmax[:, b:b + 2], src, AX.X, ALU.max, negate=True).then_inc(mx_done, 1)

            def pt_copy(v):
                un = unit(v)
                dve.wait_ge(tp_done, v + 1)
                if v >= 2:
                    dve.wait_ge(pv_done, v - 1)
                src = tbank[:].rearrange("p (h c q) -> p h c q", h=2, c=2)
                dst = PT[v % 2][:].rearrange("p (h c) q -> p h c q", h=2)
                lens = [k[3] for k in un["keys"]] if un["att"] else [P, P]
                if lens == [P, P]:
                    ins = nc.vector.tensor_copy(PT[v % 2][:].rearrange("p a q -> p (a q)"), tbank[:])
                else:
                    for c, ln in enumerate(lens):
                        ins = nc.vector.tensor_copy(dst[0:ln, :, c, :], src[0:ln, :, c, :])
                ins.then_inc(pt_done, 1)

            def lse_copy(v):
                un = unit(v)
                dve.wait_ge(ls_done, v + 1)
                if units[v][1] == 3 and units[v][2] == 0:
                    dve.wait_ge(c_bc, 9)
                nc.vector.tensor_copy(LS[:, un["g"], tok(None, un["base"], un["st"])],
                                      obank[0:2, 256:256 + P]).then_inc(ls_copied, 1)

            def combine(pr, stage):
                last = 30 * (pr + 1)
                if stage == 0:
                    dve.wait_ge(ls_copied, last)
                    step(nc.vector.tensor_tensor(vsum[:], LS[:, 0, :], LS[:, 1, :], ALU.max))
                    step(nc.vector.tensor_tensor(vsum[:], vsum[:], LS[:, 2, :], ALU.max))
                    for g in range(3):
                        nc.vector.tensor_tensor(LS[:, g, :], LS[:, g, :], vsum[:], ALU.subtract).then_inc(c_dsub, 1)
                elif stage == 1:
                    dve.wait_ge(c_exp, 3 * pr + 3)
                    step(nc.vector.tensor_tensor(vsum[:], LS[:, 0, :], LS[:, 1, :], ALU.add))
                    nc.vector.tensor_tensor(vsum[:], vsum[:], LS[:, 2, :], ALU.add).then_inc(c_sum, 1)
                elif stage == 2:
                    dve.wait_ge(c_inv, pr + 1)
                    for g in range(3):
                        ins = nc.vector.tensor_tensor(LS[:, g, :], LS[:, g, :], vsum[:], ALU.mult)
                    ins.then_inc(c_w, 1)
                else:
                    dve.wait_ge(o_copied, last)
                    for n, (t0, nt) in enumerate(SEGS):
                        for g in range(3):
                            dve.wait_ge(c_bc, 9 * pr + 3 * n + g + 1)
                            ot = OT[:, g, t0:t0 + nt]
                            nc.vector.tensor_tensor(ot, ot, w_bank[g][:, 0:nt], ALU.mult).then_inc(c_bu, 1)
                        dve.wait_ge(c_bu, 9 * pr + 3 * n + 3)
                        step(nc.vector.tensor_tensor(oB[:, pr, t0:t0 + nt], OT[:, 0, t0:t0 + nt],
                                                     OT[:, 1, t0:t0 + nt], ALU.add))
                        ins = nc.vector.tensor_tensor(oB[:, pr, t0:t0 + nt], oB[:, pr, t0:t0 + nt],
                                                      OT[:, 2, t0:t0 + nt], ALU.add)
                    ins.then_inc(c_done, 1)

            def units_steps(acts):
                for what, v in acts:
                    if what == "scores":
                        biased_max(v)
                    elif what == "lse":
                        lse_copy(v)
                    elif what == "transposes":
                        pt_copy(v)

            split_lo(0)
            rounds_done = [0]
            for t, tk in enumerate(ticks):
                s = tk["seg"]
                units_steps(tk["amid"])
                if t >= 1 and t - 1 < NSEG:
                    finish(t - 1)
                if s is not None and segs[s]["first"]:
                    split_lo(segs[s]["chunk"] + 1)
                for _ in tk["rounds"]:
                    v_copy(rounds_done[0])
                    rounds_done[0] += 1
                units_steps(tk["after"])
                for pr, stage in tk["combine"]:
                    combine(pr, stage)

        @block.tensor
        def _(pe):
            def product(s, ks):
                sg = segs[s]
                c = sg["chunk"]
                if sg["first"] and 0 in ks:
                    pe.wait_ge(lo_ready, c + 1)
                if s >= 3 and 0 in ks:
                    pe.wait_ge(seg_free, s - 2)
                hi, lo = (memT_hi, memT_lo) if sg["mem"] else (hT_hi, hT_lo)
                cols = slice(sg["t0"], sg["t0"] + sg["nt"])
                out = bank[s % 3][:, 0:sg["nt"]]
                for k in ks:
                    wh, wl = whi[c % NSPL][:, k, :], wlo[c % NSPL][:, k, :]
                    nc.tensor.matmul(out, wh, hi[:, k, cols], start=(k == 0), stop=False)
                    nc.tensor.matmul(out, wh, lo[:, k, cols], start=False, stop=False)
                    ins = nc.tensor.matmul(out, wl, hi[:, k, cols], start=False, stop=(k == KD - 1))
                if KD - 1 in ks:
                    ins.then_inc(seg_done, 1)

            def square_sums(s):
                m = norm_no[s]
                sg = segs[s]
                pe.wait_ge(sq_ready, m + 1)
                if m >= 1:
                    pe.wait_ge(lnexp, 2 * m - 1)
                if bc_before(s):
                    pe.wait_ge(c_bu, bc_before(s))
                w = ones if sg["place"][0] in ("memk", "xq") else pair_ones
                nc.tensor.matmul(misc[:, 0:sg["nt"]], w[:], sq[m % 2][:, 0:sg["nt"]], start=True,
                                 stop=True).then_inc(ss_done, 1)

            def bc_before(s):
                return 9 * sum(1 for tk in ticks[:s + 1] for _, stage in tk["combine"] if stage == 3)

            def v_round(n):
                (kind, m), tl = round_list[n]
                pe.wait_ge(seg_free, order[(kind, m)] + 1)
                free_tbank(("v", n))
                for a, (i, base, st, ln) in enumerate(tl):
                    ins = nc.tensor.transpose(tbank[0:ln, a * P:(a + 1) * P], vT[:, tok(None, base, st, ln)],
                                              ident[:])
                ins.then_inc(s_vtr, 1)

            def free_tbank(use):
                n = use_no[use]
                if n >= 1:
                    kind, i = t_use[n - 1]
                    pe.wait_ge(s_vcp if kind == "v" else pt_done, i + 1)

            def scores(v):
                un = unit(v)
                if v >= 1:
                    pe.wait_ge(mx_done if units[v - 1][0] == "att" else ex_done, v)
                if broadcast[0]:
                    pe.wait_ge(c_bu, broadcast[0])
                if un["att"]:
                    if units[v][2] == 0:
                        pe.wait_ge(seg_free, order[("k", un["ph"])] + 1)
                    q, k = qT[un["buf"]], kT[un["buf"]]
                    k0 = un["keys"][0][1]
                    for h in range(2):
                        r = slice(64 * h, 64 * h + 64)
                        ins = nc.tensor.matmul(s_bank[h][:, 0:un["nk"]], q[r, tok(None, un["base"], un["st"])],
                                               k[r, tok(None, k0, un["st"], un["nk"])], start=True, stop=True)
                else:
                    if units[v][2] == 0:
                        pe.wait_ge(seg_free, order[("xq", un["j"])] + 1)
                    pe.wait_ge(s_memin, 32)
                    for h in range(2):
                        t = 2 * un["t"] + h
                        m0 = 0 if t < 2 else 256
                        ins = nc.tensor.matmul(s_bank[h][:, 0:256], xq[un["j"]][:, t * P:(t + 1) * P],
                                               Kx[:, un["j"], m0:m0 + 256], start=True, stop=True)
                ins.then_inc(sc_done, 1)

            def lse_rows(v):
                b = 2 * (v % 3)
                pe.wait_ge(s_lse, v + 1)
                if values_issued[0]:
                    pe.wait_ge(o_copied, values_issued[0])
                if v >= 1:
                    pe.wait_ge(ls_copied, v)
                nc.tensor.transpose(obank[0:2, 256:256 + P], lse[:, b:b + 2], ident[:]).then_inc(ls_done, 1)

            def transposes(v):
                un = unit(v)
                pe.wait_ge(p_norm, v + 1)
                free_tbank(("u", v))
                lens = [k[3] for k in un["keys"]] if un["att"] else [P, P]
                for h in range(2):
                    c0 = 0
                    for c, ln in enumerate(lens):
                        ins = nc.tensor.transpose(tbank[0:ln, (2 * h + c) * P:(2 * h + c + 1) * P],
                                                  Pm[v % 3][:, h, c0:c0 + ln], ident[:])
                        c0 += ln
                ins.then_inc(tp_done, 1)

            def pv(v):
                un = unit(v)
                pe.wait_ge(pt_done, v + 1)
                if v >= 1:
                    pe.wait_ge(o_copied, v)
                if v < N_ATT:
                    pe.wait_ge(ls_copied, min(v + 2, N_ATT) if lse_issued[0] > v + 1 else v + 1)
                if un["att"] and units[v][2] == 0:
                    wait_rounds_done(pe, ("v", un["ph"]))
                for h in range(2):
                    if un["att"]:
                        for c, (i, _, _, ln) in enumerate(un["keys"]):
                            ins = nc.tensor.matmul(obank[64 * h:64 * h + 64, 0:P],
                                                   V[un["buf"]][0:ln, i, 64 * h:64 * h + 64],
                                                   PT[v % 2][0:ln, 2 * h + c, :], start=(c == 0),
                                                   stop=(c == len(un["keys"]) - 1))
                    else:
                        t = 2 * un["t"] + h
                        m0 = 0 if t < 2 else 2
                        for c in range(2):
                            ins = nc.tensor.matmul(obank[:, h * P:(h + 1) * P],
                                                   Vx[:, m0 + c, un["j"] * P:(un["j"] + 1) * P],
                                                   PT[v % 2][:, 2 * h + c, :], start=(c == 0), stop=(c == 1))
                ins.then_inc(pv_done, 1)
                values_issued[0] += 1

            def broadcasts(pr, t):
                pe.wait_ge(c_w, pr + 1)
                ns = [s for s in norm_segs if s < t]
                pe.wait_ge(lnexp, 2 * len(ns) - 1)
                pe.wait_ge(mx_done, sum(1 for tk in ticks[:t + 1] for w, _ in tk["amid"] + tk["after"]
                                        if w == "scores"))
                for n, (t0, nt) in enumerate(SEGS):
                    for g in range(3):
                        i = 9 * pr + 3 * n + g
                        if i >= 3:
                            pe.wait_ge(c_bu, i - 2)
                        nc.tensor.matmul(w_bank[g][:, 0:nt], head_rows[:], LS[:, g, t0:t0 + nt], start=True,
                                         stop=True).then_inc(c_bc, 1)
                broadcast[0] = 9 * (pr + 1)

            rounds_done = [0]
            lse_issued = [0]
            broadcast = [0]
            values_issued = [0]

            def units_steps(acts):
                for what, v in acts:
                    lse_issued[0] += what == "lse"
                    {"lse": lse_rows, "scores": scores, "transposes": transposes, "values": pv}[what](v)

            for t, tk in enumerate(ticks):
                if tk["seg"] is not None:
                    product(tk["seg"], range(MID))
                if t >= 1 and t - 1 in norm_no:
                    square_sums(t - 1)
                units_steps(tk["amid"])
                if tk["seg"] is not None:
                    product(tk["seg"], range(MID, KD))
                for _ in tk["rounds"]:
                    v_round(rounds_done[0])
                    rounds_done[0] += 1
                units_steps(tk["after"])
                for pr, stage in tk["combine"]:
                    if stage == 3:
                        broadcasts(pr, t)
    oA = at("oA", [P, NCC, NT], F32, W + 20480)
    ccs = at("ccs", [P, NT], F32, W + 51200)
    NU = NT + 4
    u = at("u", [P, NU], F32, W + 56320)
    cv = at("cv", [P, NT], F32, W + 61472)
    U0 = (1, NP_ + 3, NP_ + 3 + 512)
    S_CONV = NSEG
    cv_step = sem("conv_step")
    sp_passed = sem("passed_by_sync")
    pool_passed = sem("passed_by_pool")
    dve_passed = sem("passed_by_vector")
    CV_STEPS = 3

    def wait(eng, semaphore, value):
        if not (isinstance(value, int) and value <= 0):
            eng.wait_ge(semaphore, value)

    def wait_apart(eng, semaphore, value, passed):
        wait(eng, semaphore, value)
        eng.sem_inc(passed, 1)

    def split_lo(dve, j, c):
        dve.wait_ge(hi_ready, c + 1)
        nc.vector.tensor_tensor(wlo[j % NSPL][:], raw[j % NRAW][:], whi[j % NSPL][:].bitcast(F32),
                                ALU.subtract).then_inc(lo_ready, 1)

    assert C_CONV % 6 == 0 and C_GATE % 6 == 0

    with nc.Block() as block:
        @block.sync
        def _(sp):
            def load_after(i, j):
                wait_apart(sp, lo_ready, C_CONV + 6 * i + j + 1, sp_passed)
                n = j + NRAW
                src = conv_src(2 * i + n // 3, n % 3) if n < 6 or not (isinstance(i, int) and i == 2) else \
                    gate_src(0, n - 6)
                sp.dma_start(raw[j % NRAW][:], src).then_inc(raw_loaded[j % NRAW], 16)

            with sp.Fori(0, 2) as i:
                for j in range(6):
                    load_after(i, j)
            for j in range(6):
                load_after(2, j)

        @block.scalar
        def _(act):
            with act.Fori(0, 3) as i:
                for j in range(6):
                    act.wait_ge(seg_done, S_CONV + 18 * i + 3 * j)
                    jn = j + 1
                    act.wait_ge(raw_loaded[jn % NRAW], 16 * (C_CONV // NRAW + 2 * i + jn // NRAW + 1))
                    nc.scalar.activation(whi[jn % NSPL][:], raw[jn % NRAW][:], ACT.Copy).then_inc(hi_ready, 1)

        @block.vector
        def _(dve):
            for a in (0, NP_ + 1, NU - 1):
                n = 2 if a == NP_ + 1 else 1
                nc.vector.memset(u[:, a:a + n], 0.0).then_inc(d_chain, 1)
            with dve.Fori(0, 3) as i:
                for j in range(6):
                    ch, part, seg0 = 2 * i + j // 3, j % 3, S_CONV + 18 * i + 3 * j
                    split_lo(dve, j + 1, C_CONV + 6 * i + j + 1)
                    for n, (t0, nt) in enumerate(SEGS):
                        dve.wait_ge(seg_done, seg0 + n + 1)
                        src = bank[(S_CONV + n) % 3][:, 0:nt]
                        if part == 0:
                            dve.wait_ge(seg_free, seg0 + n)
                            nc.vector.tensor_copy(ccs[:, t0:t0 + nt], src).then_inc(seg_free, 1)
                        elif part == 1:
                            dve.wait_ge(seg_free, seg0 - 3 + n + 1)
                            nc.vector.tensor_tensor(u[:, U0[n]:U0[n] + nt], src, ccs[:, t0:t0 + nt],
                                                    ALU.mult).then_inc(seg_free, 1)
                        else:
                            if n == 0:
                                dve.wait_ge(seg_free, seg0)
                                step0 = (2 * i + j // 3) * CV_STEPS
                                for tap in range(3):
                                    w = cwc[:, bass.ds(tap * NCC + ch, 1)]
                                    for a, b0, ln in ((0, 1, NP_), (NP_, NP_ + 3, NS_)):
                                        src_u = u[:, b0 + tap - 1:b0 + tap - 1 + ln]
                                        if tap == 0:
                                            ins = nc.vector.tensor_scalar(cv[:, a:a + ln], src_u, w, None, ALU.mult)
                                        else:
                                            ins = nc.vector.scalar_tensor_tensor(cv[:, a:a + ln], src_u, w,
                                                                                 cv[:, a:a + ln], ALU.mult, ALU.add)
                                    ins.then_inc(cv_step, 1)
                                    dve.wait_ge(cv_step, step0 + tap + 1)
                            nc.vector.tensor_tensor(oA[:, bass.ds(ch, 1), t0:t0 + nt].rearrange("p a t -> p (a t)"),
                                                    src, cv[:, t0:t0 + nt], ALU.mult).then_inc(seg_free, 1)

        @block.tensor
        def _(pe):
            with pe.Fori(0, 3) as i:
                for j in range(6):
                    pe.wait_ge(lo_ready, C_CONV + 6 * i + j + 1)
                    for n, (t0, nt) in enumerate(SEGS):
                        seg = S_CONV + 18 * i + 3 * j + n
                        pe.wait_ge(seg_free, seg - 2)
                        out = bank[(S_CONV + n) % 3][:, 0:nt]
                        for k in range(KD):
                            wh, wl = whi[j % NSPL][:, k, :], wlo[j % NSPL][:, k, :]
                            nc.tensor.matmul(out, wh, hT_hi[:, k, t0:t0 + nt], start=(k == 0), stop=False)
                            nc.tensor.matmul(out, wh, hT_lo[:, k, t0:t0 + nt], start=False, stop=False)
                            ins = nc.tensor.matmul(out, wl, hT_hi[:, k, t0:t0 + nt], start=False,
                                                   stop=(k == KD - 1))
                        ins.then_inc(seg_done, 1)

    scratch_g = nc.dram_tensor("scratch_g", [3 * KD, P, NT], F32, kind="Internal").ap()
    sig = [at(f"sig{b}", [P, NT], F32, W + 51200 + 5120 * b) for b in range(3)]
    NKT = NCC + 2 + XH
    EARLY = 3
    WB = HT + 5120 * (NKT - EARLY)
    o_hi = [at(f"o_hi{k}", [P, NT], F32R, W + 66560 + 5120 * k if k < EARLY else HT + 5120 * (k - EARLY))
            for k in range(NKT)]
    o_f = [t[:, k, :] for t, n in ((oA, NCC), (oB, 2), (oC, XH)) for k in range(n)]
    o_lo = [at(f"o_lo{k}", [P, NT], F32R, place + 5120 * i)
            for k, (place, i) in enumerate([(W + 20480, i) for i in range(NCC)] + [(OB, i) for i in range(2)] +
                                           [(W, i) for i in range(XH)])]
    g_free = sem("gate_read")
    gate_done = sem("gate_done")
    sig_saved = [sem(f"gate_saved{b}") for b in range(3)]
    o_h = sem("branch_outputs_hi")
    o_l = sem("branch_outputs_lo")

    def split_outputs_hi(act, ks):
        for k in ks:
            nc.scalar.activation(o_hi[k][:], o_f[k], ACT.Copy).then_inc(o_h, 1)

    def split_outputs_lo(dve, ks):
        for k in ks:
            dve.wait_ge(o_h, k + 1)
            nc.vector.tensor_tensor(o_lo[k][:], o_f[k], o_hi[k][:].bitcast(F32), ALU.subtract).then_inc(o_l, 1)

    with nc.Block() as block:
        @block.sync
        def _(sp):
            def body(i, last):
                for j in range(6):
                    if not (last and j >= 3):
                        wait_apart(sp, lo_ready, C_GATE + 6 * i + j + 1, sp_passed)
                        n = j + NRAW
                        sp.dma_start(raw[j % NRAW][:], gate_src(2 * i + n // 3, n % 3)).then_inc(
                            raw_loaded[j % NRAW], 16)
                    wait_apart(sp, g_free, 18 * i + 3 * j + 3, sp_passed)
                    sp.dma_start(scratch_g[bass.ds(6 * i + j, 1)].rearrange("a p t -> p (a t)"),
                                 sig[j % 3][:]).then_inc(sig_saved[j % 3], 16)

            body(0, False)
            with sp.Fori(1, 3) as i:
                body(i, False)
            body(3, True)

        @block.scalar
        def _(act):
            def body(i, last):
                for j in range(6):
                    jn = j + 1
                    if not (last and j == 5):
                        wait(act, gate_done, 18 * i + 3 * j)
                        act.wait_ge(raw_loaded[jn % NRAW], 16 * (C_GATE // NRAW + 2 * i + jn // NRAW + 1))
                        nc.scalar.activation(whi[jn % NSPL][:], raw[jn % NRAW][:], ACT.Copy).then_inc(hi_ready, 1)
                    wait(act, sig_saved[j % 3], 16 * (2 * i + j // 3))
                    for n, (t0, nt) in enumerate(SEGS):
                        act.wait_ge(gate_done, 18 * i + 3 * j + n + 1)
                        nc.scalar.activation(sig[j % 3][:, t0:t0 + nt], bank[n][:, 0:nt],
                                             ACT.Sigmoid).then_inc(g_free, 1)

            body(0, False)
            split_outputs_hi(act, range(EARLY))
            with act.Fori(1, 3) as i:
                body(i, False)
            body(3, True)

        @block.vector
        def _(dve):
            with dve.Fori(0, 3) as i:
                for j in range(6):
                    split_lo(dve, j + 1, C_GATE + 6 * i + j + 1)
            for j in range(5):
                split_lo(dve, j + 1, C_GATE + 6 * 3 + j + 1)
            split_outputs_lo(dve, range(EARLY))

        @block.tensor
        def _(pe):
            def body(i):
                for j in range(6):
                    pe.wait_ge(lo_ready, C_GATE + 6 * i + j + 1)
                    for n, (t0, nt) in enumerate(SEGS):
                        wait(pe, g_free, 18 * i + 3 * j + n - 2)
                        out = bank[n][:, 0:nt]
                        for k in range(KD):
                            wh, wl = whi[j % NSPL][:, k, :], wlo[j % NSPL][:, k, :]
                            nc.tensor.matmul(out, wh, hT_hi[:, k, t0:t0 + nt], start=(k == 0), stop=False)
                            nc.tensor.matmul(out, wh, hT_lo[:, k, t0:t0 + nt], start=False, stop=False)
                            ins = nc.tensor.matmul(out, wl, hT_hi[:, k, t0:t0 + nt], start=False,
                                                   stop=(k == KD - 1))
                        ins.then_inc(gate_done, 1)

            body(0)
            with pe.Fori(1, 4) as i:
                body(i)

    wbr = [at(f"wbr{i}", [P, NKT, P], F32, WB + 6144 * i) for i in range(2)]
    wbr_hi = [at(f"wbr_hi{i}", [P, NKT, P], F32R, WB + 12288 + 6144 * i) for i in range(2)]
    wbr_lo = [at(f"wbr_lo{i}", [P, NKT, P], F32R, WB + 24576 + 6144 * i) for i in range(2)]
    acc = [at(f"acc{i}", [P, NT], F32, WB + 36864 + 5120 * i) for i in range(2)]
    tmp = at("tmp", [P, NT], F32, WB + 47104)
    assert WB + 52224 <= OB
    BR = ((0, NCC, w_bc), (NCC, 2, w_ba), (NCC + 2, XH, w_bx))
    wbr_loaded = [sem(f"wbr_loaded{i}") for i in range(2)]
    wbr_h = sem("wbr_hi_ready")
    wbr_l = sem("wbr_lo_ready")
    sig_loaded = [sem(f"gate_loaded{b}") for b in range(3)]
    y_done = sem("branch_done")
    y_free = sem("branch_read")
    acc_step = sem("acc_step")
    m_saved = [sem(f"merged_saved{i}") for i in range(2)]

    def run_tiles(eng, body):
        for h in range(2):
            body(h, h, 0)
        with eng.Fori(1, KD // 2 - 1) as i:
            for h in range(2):
                body(2 * i + h, h, i)
        for h in range(2):
            body(KD - 2 + h, h, KD // 2 - 1)

    def before(m, last):
        return not isinstance(m, int) or m < last

    with nc.Block() as block:
        @block.sync
        def _(sp):
            def load_wbr(m, h):
                for (k0, nk, w) in BR:
                    sp.dma_start(wbr[h][:, k0:k0 + nk, :], cols_of(w, P * m)).then_inc(wbr_loaded[h], 16)

            def load_sig(m, b):
                sp.dma_start(sig[b][:], scratch_g[bass.ds(3 * m + b, 1)].rearrange("a p t -> p (a t)")).then_inc(
                    sig_loaded[b], 16)

            def body(m, h, i):
                if before(m, KD - 2):
                    wait_apart(sp, wbr_l, m + 1, sp_passed)
                    load_wbr(m + 2, h)
                if before(m, KD - 1):
                    for b in range(3):
                        wait_apart(sp, y_free, 9 * m + 3 * b + 3, sp_passed)
                        load_sig(m + 1, b)
                wait_apart(sp, acc_step, 2 * m + 2, sp_passed)
                sp.dma_start(scratch_m[bass.ds(m, 1)].rearrange("a p t -> p (a t)"),
                             acc[h][:]).then_inc(m_saved[h], 16)

            for h in range(2):
                load_wbr(h, h)
                for b in range(3 if h == 0 else 0):
                    sp.wait_ge(sig_saved[b], 16 * KD)
                    load_sig(0, b)
            run_tiles(sp, body)

        @block.scalar
        def _(act):
            def weights_hi(m, h, i):
                act.wait_ge(wbr_loaded[h], 48 * i + 48)
                nc.scalar.activation(wbr_hi[h][:], wbr[h][:], ACT.Copy).then_inc(wbr_h, 1)

            def body(m, h, i):
                if before(m, KD - 1):
                    wait(act, y_done, 9 * m)
                    weights_hi(m + 1, 1 - h, i + h)

            split_outputs_hi(act, range(EARLY, NCC))
            weights_hi(0, 0, 0)
            split_outputs_hi(act, range(NCC, NKT))
            run_tiles(act, body)

        @block.vector
        def _(dve):
            def weights_lo(m, h):
                dve.wait_ge(wbr_h, m + 1)
                nc.vector.tensor_tensor(wbr_lo[h][:], wbr[h][:], wbr_hi[h][:].bitcast(F32),
                                        ALU.subtract).then_inc(wbr_l, 1)

            def body(m, h, i):
                for b in range(3):
                    if b == 0:
                        wait(dve, m_saved[h], 16 * i)
                    else:
                        wait(dve, acc_step, 2 * m + b - 1)
                    dve.wait_ge(sig_loaded[b], 16 * m + 16)
                    for n, (t0, nt) in enumerate(SEGS):
                        dve.wait_ge(y_done, 9 * m + 3 * b + n + 1)
                        nc.vector.tensor_tensor((acc[h] if b == 0 else tmp)[:, t0:t0 + nt],
                                                bank[(9 * h + 3 * b + n) % 6][:, 0:nt], sig[b][:, t0:t0 + nt],
                                                ALU.mult).then_inc(y_free, 1)
                    if b > 0:
                        dve.wait_ge(y_free, 9 * m + 3 * b + 3)
                        nc.vector.tensor_tensor(acc[h][:], acc[h][:], tmp[:], ALU.add).then_inc(acc_step, 1)
                    if b == 1 and before(m, KD - 1):
                        weights_lo(m + 1, 1 - h)

            split_outputs_lo(dve, range(EARLY, NCC))
            weights_lo(0, 0)
            split_outputs_lo(dve, range(NCC, NKT))
            run_tiles(dve, body)

        @block.tensor
        def _(pe):
            def body(m, h, i):
                pe.wait_ge(wbr_l, m + 1)
                for b, (k0, nk, _w) in enumerate(BR):
                    for n, (t0, nt) in enumerate(SEGS):
                        wait(pe, y_free, 9 * m + 3 * b + n - 5)
                        out = bank[(9 * h + 3 * b + n) % 6][:, 0:nt]
                        for k in range(k0, k0 + nk):
                            if isinstance(m, int) and m == 0 and n == 0:
                                pe.wait_ge(o_l, k + 1)
                            wh, wl = wbr_hi[h][:, k, :], wbr_lo[h][:, k, :]
                            nc.tensor.matmul(out, wh, o_hi[k][:, t0:t0 + nt], start=(k == k0), stop=False)
                            nc.tensor.matmul(out, wh, o_lo[k][:, t0:t0 + nt], start=False, stop=False)
                            ins = nc.tensor.matmul(out, wl, o_hi[k][:, t0:t0 + nt], start=False,
                                                   stop=(k == k0 + nk - 1))
                        ins.then_inc(y_done, 1)

            run_tiles(pe, body)

    o = HT
    def place(name, shape, dt=F32):
        nonlocal o
        t = at(name, shape, dt, o)
        size = 4
        for n in shape[1:]:
            size *= n
        o += -(-size // 32) * 32
        return t

    affT = place("affT", [NEXP, NT])
    gates_r = [place("gates_rows_s", [NEXP, CAP_S]), place("gates_rows_p", [NEXP, CAP_P])]
    idx_r = [place("idx_rows_s", [NEXP, CAP_S]), place("idx_rows_p", [NEXP, CAP_P])]
    top8 = place("top8", [NEXP, 8])
    top8i = place("top8_idx", [NEXP, 8], U32)
    EC = 256
    NER, NES = 6, 6
    wo_raw = [at(f"wo_raw{k}", [P, D], F32, o + 4096 * k) for k in range(KD)]
    wo_loaded = [sem(f"wo_loaded{k}") for k in range(KD)]
    wo_h = sem("wo_hi_ready")
    eraw = [place(f"eraw{i}", [P, KD, EC]) for i in range(NER)]
    AFTER_RING = o
    wo_hi = place("wo_hi", [P, KD, D], F32R)
    wo_lo = place("wo_lo", [P, KD, D], F32R)
    g2b = place("g2b", [P, D])
    wr = place("wr", [P, KD, NEXP])
    mg = [place(f"mg{i}", [P, KD, P]) for i in range(2)]
    mg_hi = [place(f"mg_hi{i}", [P, KD, P], F32R) for i in range(2)]
    mg_lo = [place(f"mg_lo{i}", [P, KD, P], F32R) for i in range(2)]
    x1 = [place(f"x1{i}", [P, D]) for i in range(2)]
    tn = [place(f"tn{i}", [P, D]) for i in range(2)]
    tT = place("tT", [P, KD, P])
    expo = place("expo", [P, NEXP])
    aff = place("aff", [P, NEXP])
    st2 = place("st2", [P, 8])

    wo_l = sem("wo_lo_ready")
    s_c4 = sem("router_consts")
    mg_loaded = [sem(f"merged_loaded{i}") for i in range(2)]
    mg_h = sem("merged_hi")
    mg_l = sem("merged_lo")
    xr_loaded = [sem(f"residual_loaded{i}") for i in range(2)]
    mm4 = sem("wo_product")
    x1_ready = sem("x1_ready")
    x1_ss = sem("x1_squares")
    x1_rs = sem("x1_rstd")
    t_ready = sem("t_ready")
    t_tr = sem("t_transposed")
    t_cp = sem("tT_copied")
    lg_done = sem("logits")
    lg_max = sem("logits_max")
    lg_exp = sem("logits_exp")
    lg_inv = sem("logits_inverse")
    af_ready = sem("affinities")
    af_tr = sem("affinities_transposed")
    af_cp = sem("affinities_copied")
    x1_saved = [sem(f"x1_saved{i}") for i in range(2)]
    t_saved = [sem(f"t_saved{i}") for i in range(2)]
    er_loaded = [sem(f"expert_raw_loaded{i}") for i in range(NER)]

    mats = [("g", 0), ("u", 0), ("g", 1), ("u", 1), ("g", 2), ("u", 2), ("g", 3), ("u", 3),
            ("d", 0), ("d", 1), ("d", 2), ("d", 3)]
    NCH = len(mats)

    def expert_src(e, j):
        what, c = mats[j]
        w = {"g": w_eg, "u": w_eu, "d": w_ed}[what]
        return w[bass.ds(e, 1), :, c * EC:(c + 1) * EC].rearrange("a (k p) n -> p (a k) n", p=P)

    tk = sem("topk_step")
    ROUNDS_P, ROUNDS_S = CAP_P // 8, CAP_S // 8

    def topk_round(dve, s, r, first):
        t0, nt = ((NP_, NS_), (0, NP_))[s]
        row = affT[:, t0:t0 + nt]
        wait_apart(dve, tk, first + 3 * r, dve_passed)
        nc.vector.max(top8[:], row).then_inc(tk, 1)
        dve.wait_ge(tk, first + 3 * r + 1)
        nc.vector.tensor_copy(gates_r[s][:, bass.ds(8 * r, 8)], top8[:])
        nc.vector.max_index(top8i[:], top8[:], row).then_inc(tk, 1)
        dve.wait_ge(tk, first + 3 * r + 2)
        nc.vector.tensor_scalar(idx_r[s][:, bass.ds(8 * r, 8)], top8i[:], float(t0), None, ALU.add)
        nc.vector.match_replace(row, top8[:], row, -1.0).then_inc(tk, 1)

    N4 = NT // P

    def stages(eng, body):
        def peeled(n):
            body(n, n % 2, n // 2, n < N4, 1 <= n <= N4, n >= 2)

        for n in range(4):
            peeled(n)
        with eng.Fori(2, N4 // 2 - 1) as i:
            for h in range(2):
                body(2 * i + h, h, i, True, True, True)
        for n in range(N4 - 2, N4 + 2):
            peeled(n)

    def split_next(n):
        return not isinstance(n, int) or 1 <= n < N4 - 1

    with nc.Block() as block:
        @block.sync
        def _(sp):
            for k in range(KD):
                sp.dma_start(wo_raw[k][:], w_o[k * P:(k + 1) * P, :]).then_inc(wo_loaded[k], 16)
                if k == 1:
                    for h in range(2):
                        sp.wait_ge(m_saved[h], 16 * (KD // 2))
                if k in (1, KD - 1):
                    n = k // 4
                    sp.dma_start(mg[n][:], scratch_m[:, :, n * P:(n + 1) * P].rearrange(
                        "k p t -> p k t")).then_inc(mg_loaded[n], 16)
            for n in range(2):
                sp.dma_start(x1[n][:], x[n * P:(n + 1) * P, :]).then_inc(xr_loaded[n], 16)
            sp.dma_start(g2b[:], g2.rearrange("(a n) -> a n", a=1).to_broadcast([P, D])).then_inc(s_c4, 16)
            sp.dma_start(wr[:], w_r.rearrange("(k p) n -> p k n", p=P)).then_inc(s_c4, 16)
            def load(n, h, sixteens):
                sp.wait_ge(mg_l, n - 1)
                sp.dma_start(mg[h][:], scratch_m[:, :, bass.ds(P * n, P)].rearrange(
                    "k p t -> p k t")).then_inc(mg_loaded[h], 16)
                wait_apart(sp, t_ready, n - 1, sp_passed)
                sp.wait_ge(x1_saved[h], sixteens)
                sp.dma_start(x1[h][:], x[bass.ds(P * n, P), :]).then_inc(xr_loaded[h], 16)

            with sp.Fori(1, N4 // 2) as i:
                for h in range(2):
                    load(2 * i + h, h, 16 * i)

        @block.gpsimd
        def _(pool):
            with pool.Fori(0, N4 // 2) as i:
                for h in range(2):
                    n = 2 * i + h
                    pool.wait_ge(x1_ready, n + 1)
                    pool.dma_start(y[bass.ds(P * n, P), :], x1[h][:]).then_inc(x1_saved[h], 16)
                    wait_apart(pool, t_ready, n + 1, pool_passed)
                    pool.dma_start(scratch_t[bass.ds(P * n, P), :], tn[h][:]).then_inc(t_saved[h], 16)

        @block.scalar
        def _(act):
            nc.scalar.preload_act_table_set("natural_log_exp_and_others")
            for h in range(2):
                act.wait_ge(m_saved[h], 16 * (KD // 2))
            for k in range(KD):
                act.wait_ge(wo_loaded[k], 16)
                nc.scalar.activation(wo_hi[:, k, :], wo_raw[k][:], ACT.Copy).then_inc(wo_h, 1)
                if k in (1, KD - 1):
                    n = k // 4
                    act.wait_ge(mg_loaded[n], 16)
                    nc.scalar.activation(mg_hi[n][:], mg[n][:], ACT.Copy).then_inc(mg_h, 1)

            def body(n, h, i, now, one, two):
                if split_next(n):
                    act.wait_ge(mm4, n)
                    act.wait_ge(mg_loaded[1 - h], 16 * (i + 1 + h))
                    nc.scalar.activation(mg_hi[1 - h][:], mg[1 - h][:], ACT.Copy).then_inc(mg_h, 1)
                if one:
                    act.wait_ge(t_tr, n)
                    wait(act, lg_done, n - 1)
                    nc.scalar.activation(tT[:].rearrange("p k t -> p (k t)"),
                                         pair_bank[:].rearrange("p a b -> p (a b)"), ACT.Copy).then_inc(t_cp, 1)
                if now:
                    act.wait_ge(x1_ready, n + 1)
                    wait(act, t_tr, n - 1)
                    wait(act, t_saved[h], 16 * i)
                    nc.scalar.activation(tn[h][:], x1[h][:], ACT.Square,
                                         accum_out=st2[:, h:h + 1]).then_inc(x1_ss, 1)
                    act.wait_ge(x1_ss, n + 1)
                    nc.scalar.activation(st2[:, h:h + 1], st2[:, h:h + 1], ACT.Ln, bias=eps_d[:, 0:1],
                                         scale=1.0 / D).then_inc(x1_rs, 1)
                    act.wait_ge(x1_rs, 2 * n + 1)
                    nc.scalar.activation(st2[:, h:h + 1], st2[:, h:h + 1], ACT.Exp, scale=-0.5).then_inc(x1_rs, 1)
                if one:
                    act.wait_ge(lg_max, n)
                    wait(act, af_ready, n - 1)
                    nc.scalar.activation(expo[:], bank[4][:, 0:NEXP], ACT.Exp, bias=st2[:, 2:3],
                                         accum_out=st2[:, 3:4]).then_inc(lg_exp, 1)

            stages(act, body)

        @block.vector
        def _(dve):
            for k in range(KD):
                if k in (2, KD - 1):
                    n = k // 4
                    dve.wait_ge(mg_h, n + 1)
                    nc.vector.tensor_tensor(mg_lo[n][:], mg[n][:], mg_hi[n][:].bitcast(F32),
                                            ALU.subtract).then_inc(mg_l, 1)
                dve.wait_ge(wo_h, k + 1)
                nc.vector.tensor_tensor(wo_lo[:, k, :], wo_raw[k][:], wo_hi[:, k, :].bitcast(F32),
                                        ALU.subtract).then_inc(wo_l, 1)
            dve.wait_ge(s_c4, 32)
            nc.vector.memset(top8[:], 0.0).then_inc(tk, 1)

            def body(n, h, i, now, one, two):
                if split_next(n):
                    dve.wait_ge(mg_h, n + 2)
                    nc.vector.tensor_tensor(mg_lo[1 - h][:], mg[1 - h][:], mg_hi[1 - h][:].bitcast(F32),
                                            ALU.subtract).then_inc(mg_l, 1)
                if two:
                    dve.wait_ge(af_tr, n - 1)
                    nc.vector.tensor_copy(affT[:, bass.ds(P * (n - 2), P)], bank[5][0:NEXP, 0:P]).then_inc(af_cp, 1)
                if now:
                    dve.wait_ge(mm4, n + 1)
                    dve.wait_ge(xr_loaded[h], 16 * i + 16)
                    for a in range(2):
                        cols = slice(512 * a, 512 * a + 512)
                        ins = nc.vector.tensor_tensor(x1[h][:, cols], bank[2 * h + a][:], x1[h][:, cols], ALU.add)
                    ins.then_inc(x1_ready, 1)
                if now:
                    dve.wait_ge(x1_rs, 2 * n + 2)
                    nc.vector.scalar_tensor_tensor(tn[h][:], x1[h][:], st2[:, h:h + 1], g2b[:], ALU.mult,
                                                   ALU.mult).then_inc(t_ready, 1)
                if one:
                    dve.wait_ge(lg_done, n)
                    wait(dve, lg_exp, n - 1)
                    nc.vector.tensor_reduce(st2[:, 2:3], bank[4][:, 0:NEXP], AX.X, ALU.max,
                                            negate=True).then_inc(lg_max, 1)
                    dve.wait_ge(lg_exp, n)
                    nc.vector.reciprocal(st2[:, 4:5], st2[:, 3:4]).then_inc(lg_inv, 1)
                    dve.wait_ge(lg_inv, n)
                    wait(dve, af_tr, n - 1)
                    nc.vector.tensor_scalar(aff[:], expo[:], st2[:, 4:5], None, ALU.mult).then_inc(af_ready, 1)
                if isinstance(n, int) and n in (N4 - 2, N4 - 1):
                    dve.wait_ge(af_cp, NP_ // P)
                    for r in range(ROUNDS_P // 2):
                        topk_round(dve, 1, (n - (N4 - 2)) * (ROUNDS_P // 2) + r, 1)

            stages(dve, body)

        @block.tensor
        def _(pe):
            def body(n, h, i, now, one, two):
                def half(a):
                    cols = slice(512 * a, 512 * a + 512)
                    out = bank[2 * h + a][:]
                    for k in range(KD):
                        if isinstance(n, int) and n == 0 and a == 0:
                            pe.wait_ge(wo_l, k + 1)
                        nc.tensor.matmul(out, mg_hi[h][:, k, :], wo_hi[:, k, cols], start=(k == 0), stop=False)
                        nc.tensor.matmul(out, mg_hi[h][:, k, :], wo_lo[:, k, cols], start=False, stop=False)
                        ins = nc.tensor.matmul(out, mg_lo[h][:, k, :], wo_hi[:, k, cols], start=False,
                                               stop=(k == KD - 1))
                    return ins

                if now:
                    pe.wait_ge(mg_l, n + 1)
                    wait(pe, x1_ready, n - 1)
                    half(0)
                if one:
                    pe.wait_ge(t_ready, n)
                    wait(pe, t_cp, n - 1)
                    for k in range(KD):
                        ins = nc.tensor.transpose(pair_bank[:, k // 4, (k % 4) * P:(k % 4 + 1) * P],
                                                  tn[1 - h][:, k * P:(k + 1) * P], ident[:])
                    ins.then_inc(t_tr, 1)
                if two:
                    pe.wait_ge(af_ready, n - 1)
                    wait(pe, af_cp, n - 2)
                    nc.tensor.transpose(bank[5][0:NEXP, 0:P], aff[:], ident[:]).then_inc(af_tr, 1)
                if now:
                    half(1).then_inc(mm4, 1)
                if one:
                    if isinstance(n, int) and n == 1:
                        pe.wait_ge(s_c4, 32)
                    pe.wait_ge(t_cp, n)
                    wait(pe, af_ready, n - 1)
                    for k in range(KD):
                        ins = nc.tensor.matmul(bank[4][:, 0:NEXP], tT[:, k, :], wr[:, k, :], start=(k == 0),
                                               stop=(k == KD - 1))
                    ins.then_inc(lg_done, 1)

            stages(pe, body)

    o = AFTER_RING
    ehi = [place(f"ehi{i}", [P, KD, EC], F32R) for i in range(NES)]
    elo = [place(f"elo{i}", [P, KD, EC], F32R) for i in range(NES)]
    xp = place("tokens_hi_lo", [P, KD, 2 * CAP], F32R)
    hid = place("hidden_hi_lo", [P, KD, 2 * CAP], F32R)
    HI, LO = slice(0, CAP), slice(CAP, 2 * CAP)
    low = [place(f"low_product{i}", [P, 2, CAP]) for i in range(2)]
    gate_sum = place("gate_sum", [P, 2, CAP])
    up_sum = place("up_sum", [P, 2, CAP])
    sg = place("silu_gate", [P, 2, CAP])
    hidf = place("hidden", [P, 2, CAP])
    yT_s = place("yT_s", [P, KD, CAP_S])
    yT_p = place("yT_p", [P, KD, CAP_P])
    PACK = P // CAP_P
    y_rows = [place("y_rows_s", [P, D]), place("y_rows_p", [P, KD // PACK * P])]
    xg = [place("x_rows_s", [P, D]), place("x_rows_p", [CAP_P, D])]
    CAPS = (CAP_S, CAP_P)
    gates_c = [place("gates_cols_s", [CAP_S, NEXP]), place("gates_cols_p", [P, NEXP])]
    gates_w = place("gates_packed", [NEXP, PACK, CAP_P])
    idx_w = place("idx_packed", [NEXP, PACK, CAP_P])
    idx_wc = place("idx_packed_cols", [P, NEXP])
    idx_c = [place("idx_cols_s", [CAP_S, NEXP], U32), place("idx_cols_p", [CAP_P, NEXP], U32)]
    g_cur = [place("gate_s", [CAP_S, 1]), place("gate_p", [P, 1])]
    iw_s = place("idx_scatter_s", [CAP_S, 1], U32)
    iw_p = [place(f"idx_scatter_p{g}", [P, 1], U32) for g in range(KD // PACK)]
    SCATTERED = (16, 16 * (KD // PACK))
    ig_cur = [place("idx_gather_s", [CAP_S, 1], U32), place("idx_gather_p", [CAP_P, 1], U32)]

    e_hi = sem("expert_hi")
    e_lo_d = sem("expert_lo_by_vector")
    e_lo_p = sem("expert_lo_by_pool")
    tk_tr = sem("topk_transposed")
    packed = sem("prompt_rows_packed")
    cols_ready = sem("topk_columns")
    ig_ready = sem("gather_index")
    iw_ready = sem("scatter_index")
    gathered = [sem("gathered_s"), sem("gathered_p")]
    scattered = [sem("scattered_s"), sem("scattered_p")]
    x_tr = sem("x_rows_transposed")
    x_hi = sem("x_tokens_hi")
    x_lo = sem("x_tokens_lo")
    mm5 = sem("expert_product")
    silu_ready = sem("silu_ready")
    h_ready = sem("hidden_ready")
    h_hi = sem("hidden_hi")
    h_lo = sem("hidden_lo")
    low_ready = sem("low_product_copied")
    summed = sem("product_summed")
    y_tr = sem("y_rows_transposed")
    y_rdy = sem("y_rows_ready")
    XB = ((0, 3), (3, 6), (6, 8))
    AHEAD = 4

    def wait_lo(eng, e, j):
        if j % 4 == 3:
            eng.wait_ge(e_lo_p, 3 * e + j // 4 + 1)
        else:
            eng.wait_ge(e_lo_d, 9 * e + j - j // 4 + 1)

    def run_experts(eng, body):
        body(0, False, True)
        body(1, True, True)
        with eng.Fori(2, NEXP - 1) as e:
            body(e, True, True)
        body(NEXP - 1, True, False)

    with nc.Block() as block:
        @block.sync
        def _(sp):
            def body(e, _before, after):
                for j in range(NCH if after else NCH - NER):
                    wait_lo(sp, e, j)
                    sp.sem_inc(sp_passed, 1)
                    jn = j + NER
                    sp.dma_start(eraw[j % NER][:], expert_src(e + jn // NCH, jn % NCH)).then_inc(
                        er_loaded[j % NER], 16)

            for c in range(NER):
                sp.dma_start(eraw[c][:], expert_src(0, c)).then_inc(er_loaded[c], 16)
            run_experts(sp, body)

        @block.gpsimd
        def _(pool):
            def gather(e):
                pool.wait_ge(ig_ready, e + 1)
                wait_apart(pool, x_tr, 3 * e, pool_passed)
                for s in range(2):
                    nc.gpsimd.indirect_dma_start(xg[s][:], None, scratch_t[:],
                                                 bass.IndirectOffsetOnAxis(ap=ig_cur[s][:], axis=0)).then_inc(
                        gathered[s], 16)

            def scatter(e):
                pool.wait_ge(iw_ready, e + 1)
                for s in range(2):
                    pool.wait_ge(y_rdy, 2 * e + s + 1)
                    wait_apart(pool, scattered[s], SCATTERED[s] * e, pool_passed)
                    if s == 0:
                        nc.gpsimd.indirect_dma_start(y[:], bass.IndirectOffsetOnAxis(ap=iw_s[:], axis=0),
                                                     y_rows[0][:], None, compute_op=ALU.add).then_inc(
                            scattered[0], 16)
                    else:
                        pieces = y.rearrange("t (k f) -> (t k) f", f=P)
                        for g in range(KD // PACK):
                            nc.gpsimd.indirect_dma_start(pieces, bass.IndirectOffsetOnAxis(ap=iw_p[g][:], axis=0),
                                                         y_rows[1][:, g * P:(g + 1) * P], None,
                                                         compute_op=ALU.add).then_inc(scattered[1], 16)

            def body(e, before, after):
                for j in range(NCH):
                    jn = j + AHEAD
                    if jn % 4 == 3 and (after or jn < NCH):
                        pool.wait_ge(e_hi, NCH * e + jn + 1)
                        nc.gpsimd.tensor_tensor(elo[jn % NES][:], eraw[jn % NER][:], ehi[jn % NES][:].bitcast(F32),
                                                ALU.subtract).then_inc(e_lo_p, 1)
                    if j == 0 and before:
                        scatter(e - 1)
                    if j == 3 and after:
                        gather(e + 1)

            pool.wait_ge(e_hi, 4)
            nc.gpsimd.tensor_tensor(elo[3][:], eraw[3][:], ehi[3][:].bitcast(F32), ALU.subtract).then_inc(e_lo_p, 1)
            for h in range(2):
                pool.wait_ge(x1_saved[h], 16 * (N4 // 2))
                pool.wait_ge(t_saved[h], 16 * (N4 // 2))
            gather(0)
            run_experts(pool, body)
            scatter(NEXP - 1)
            for s in range(2):
                pool.wait_ge(scattered[s], SCATTERED[s] * NEXP)

        @block.scalar
        def _(act):
            def hi(e, j):
                act.wait_ge(er_loaded[j % NER], 16 * (2 * e + j // NER + 1))
                nc.scalar.activation(ehi[j % NES][:], eraw[j % NER][:], ACT.Copy).then_inc(e_hi, 1)

            def x_split(e, b):
                act.wait_ge(x_tr, 3 * e + b + 1)
                k0, k1 = XB[b]
                src = bank[4 + b % 2][:, 0:(k1 - k0) * CAP].rearrange("p (k t) -> p k t", t=CAP)
                nc.scalar.activation(xp[:, k0:k1, HI], src, ACT.Copy).then_inc(x_hi, 1)

            def hidden_hi(e, q):
                act.wait_ge(h_ready, 4 * e + q + 1)
                nc.scalar.activation(hid[:, 2 * q:2 * q + 2, HI], hidf[:], ACT.Copy).then_inc(h_hi, 1)

            def y_out(e, s):
                act.wait_ge(iw_ready, e + 1)
                act.wait_ge(y_tr, 2 * e + s + 1)
                wait(act, scattered[s], SCATTERED[s] * e)
                src = pair_bank[:].rearrange("p a b -> p (a b)") if s == 0 else pair_bank[:, 0, 0:KD // PACK * P]
                nc.scalar.activation(y_rows[s][:], src, ACT.Copy, scale=g_cur[s][:, 0:1]).then_inc(y_rdy, 1)

            def body(e, before, after):
                for j in range(NCH):
                    c = NCH * e + j
                    if j == 8:
                        hidden_hi(e, 3)
                    if after or j + AHEAD < NCH:
                        wait(act, mm5, c - (NES - AHEAD) + 1)
                        hi(e, j + AHEAD)
                    if j < 8 and j % 2 == 1:
                        q = 4 * e + j // 2
                        act.wait_ge(summed, c)
                        wait(act, h_ready, q)
                        nc.scalar.activation(sg[:], gate_sum[:], ACT.Silu).then_inc(silu_ready, 1)
                    if 2 <= j < 8 and j % 2 == 0:
                        hidden_hi(e, j // 2 - 1)
                    if after and j == 10:
                        x_split(e + 1, 0)
                        x_split(e + 1, 1)
                    if after and j == 11:
                        x_split(e + 1, 2)
                    if before and j in (1, 2):
                        y_out(e - 1, j - 1)
                    act.wait_ge(mm5, c + 1)
                    wait(act, summed, c - 1)
                    nc.scalar.activation(low[j % 2][:], pairs[j % 2][:, :, LO], ACT.Copy).then_inc(low_ready, 1)

            for j in range(AHEAD):
                hi(0, j)
            for b in range(3):
                x_split(0, b)
            run_experts(act, body)
            for s in range(2):
                y_out(NEXP - 1, s)

        @block.vector
        def _(dve):
            def lo(e, j):
                dve.wait_ge(e_hi, NCH * e + j + 1)
                nc.vector.tensor_tensor(elo[j % NES][:], eraw[j % NER][:], ehi[j % NES][:].bitcast(F32),
                                        ALU.subtract).then_inc(e_lo_d, 1)

            def x_split(e, b):
                dve.wait_ge(x_hi, 3 * e + b + 1)
                k0, k1 = XB[b]
                src = bank[4 + b % 2][:, 0:(k1 - k0) * CAP].rearrange("p (k t) -> p k t", t=CAP)
                nc.vector.tensor_tensor(xp[:, k0:k1, LO], src, xp[:, k0:k1, HI].bitcast(F32),
                                        ALU.subtract).then_inc(x_lo, 1)

            def hidden_lo(e, q):
                dve.wait_ge(h_hi, 4 * e + q + 1)
                pair = hid[:, 2 * q:2 * q + 2]
                nc.vector.tensor_tensor(pair[:, :, LO], hidf[:], pair[:, :, HI].bitcast(F32),
                                        ALU.subtract).then_inc(h_lo, 1)

            def column(e):
                return bass.ds(e, 1)

            def gather_index(e):
                for s in range(2):
                    wait(dve, gathered[s], 16 * e)
                    ins = nc.vector.tensor_copy(ig_cur[s][:], idx_c[s][:, column(e)])
                ins.then_inc(ig_ready, 1)

            def scatter_index(e):
                wait(dve, y_rdy, 2 * e)
                for s in range(2):
                    wait(dve, scattered[s], SCATTERED[s] * e)
                    nc.vector.tensor_copy(g_cur[s][:], gates_c[s][:, column(e)])
                nc.vector.tensor_copy(iw_s[:], idx_c[0][:, column(e)])
                for g in range(KD // PACK):
                    ins = nc.vector.tensor_scalar(iw_p[g][:], idx_wc[:, column(e)], float(PACK * g), None, ALU.add)
                ins.then_inc(iw_ready, 1)

            def body(e, before, after):
                for j in range(NCH):
                    c = NCH * e + j
                    jn = j + AHEAD
                    if j == 8:
                        hidden_lo(e, 3)
                    if jn % 4 != 3 and (after or jn < NCH):
                        lo(e, jn)
                    if 2 <= j < 8 and j % 2 == 0:
                        hidden_lo(e, j // 2 - 1)
                    if j == 0 and before:
                        scatter_index(e - 1)
                    if j == 3 and after:
                        gather_index(e + 1)
                    if after and j == 10:
                        x_split(e + 1, 0)
                        x_split(e + 1, 1)
                    if after and j == 11:
                        x_split(e + 1, 2)
                    dve.wait_ge(low_ready, c + 1)
                    q = 4 * e + j // 2
                    src, m = pairs[j % 2], 2 * (j - 8)
                    if j >= 8:
                        if j == 8:
                            wait(dve, y_tr, 2 * e)
                        nc.vector.tensor_tensor(yT_s[:, m:m + 2, :], src[:, :, 0:CAP_S], low[j % 2][:, :, 0:CAP_S],
                                                ALU.add)
                        ins = nc.vector.tensor_tensor(yT_p[:, m:m + 2, :], src[:, :, CAP_S:CAP],
                                                      low[j % 2][:, :, CAP_S:CAP], ALU.add)
                    else:
                        wait(dve, silu_ready if j % 2 == 0 else h_ready, q)
                        ins = nc.vector.tensor_tensor((gate_sum, up_sum)[j % 2][:], src[:, :, HI], low[j % 2][:],
                                                      ALU.add)
                    ins.then_inc(summed, 1)
                    if j < 8 and j % 2 == 1:
                        dve.wait_ge(summed, c + 1)
                        dve.wait_ge(silu_ready, q + 1)
                        wait(dve, h_lo, q)
                        nc.vector.tensor_tensor(hidf[:], up_sum[:], sg[:], ALU.mult).then_inc(h_ready, 1)

            for k in range(PACK):
                nc.vector.tensor_copy(gates_w[:, k, :], gates_r[1][:])
                ins = nc.vector.tensor_scalar(idx_w[:, k, :], idx_r[1][:], float(KD), float(k), ALU.mult, ALU.add)
            ins.then_inc(packed, 1)
            with dve.Fori(0, ROUNDS_S) as r:
                topk_round(dve, 0, r, 1 + 3 * ROUNDS_P)
            dve.wait_ge(tk_tr, 1)
            for s in range(2):
                nc.vector.tensor_copy(idx_c[s][:], bank[4 + s][0:CAPS[s], 0:NEXP])
                nc.vector.tensor_copy(gates_c[s][:], bank[4 + s][:, NEXP:2 * NEXP])
            nc.vector.tensor_copy(idx_wc[:], bank[5][:, 2 * NEXP:3 * NEXP]).then_inc(cols_ready, 1)
            dve.wait_ge(cols_ready, 1)
            gather_index(0)
            lo(0, 0)
            lo(0, 1)
            for b in range(3):
                x_split(0, b)
            lo(0, 2)
            run_experts(dve, body)
            scatter_index(NEXP - 1)

        @block.tensor
        def _(pe):
            def x_rows(e, b):
                if b == 0:
                    for s in range(2):
                        pe.wait_ge(gathered[s], 16 * e + 16)
                    if isinstance(e, int) and e == 0:
                        pe.wait_ge(cols_ready, 1)
                wait(pe, x_lo, 3 * e + (b == 2))
                k0, k1 = XB[b]
                for k in range(k0, k1):
                    at_k = (k - k0) * CAP
                    f = slice(k * P, (k + 1) * P)
                    nc.tensor.transpose(bank[4 + b % 2][:, at_k:at_k + CAP_S], xg[0][:, f], ident[:])
                    ins = nc.tensor.transpose(bank[4 + b % 2][:, at_k + CAP_S:at_k + CAP], xg[1][:, f],
                                              ident[0:CAP_P, 0:CAP_P])
                ins.then_inc(x_tr, 1)

            def y_back(e, s):
                if s == 0:
                    pe.wait_ge(summed, NCH * e + NCH)
                wait(pe, y_rdy, 2 * e + s)
                if s == 0:
                    for k in range(KD):
                        ins = nc.tensor.transpose(pair_bank[:, k // 4, (k % 4) * P:(k % 4 + 1) * P],
                                                  yT_s[:, k, :], ident[:])
                else:
                    for g in range(KD // PACK):
                        four = yT_p[:, PACK * g:PACK * (g + 1), :].rearrange("p k t -> p (k t)")
                        ins = nc.tensor.transpose(pair_bank[:, 0, g * P:(g + 1) * P], four, ident[:])
                ins.then_inc(y_tr, 1)

            def product(e, j, ks):
                moving = xp if j < 8 else hid
                for m in range(2):
                    out = pairs[j % 2][:, m, 0:2 * CAP]
                    for k in ks:
                        cols = slice(m * P, (m + 1) * P)
                        wh, wl = ehi[j % NES][:, k, cols], elo[j % NES][:, k, cols]
                        nc.tensor.matmul(out, wh, moving[:, k, :], start=(k == 0), stop=False)
                        ins = nc.tensor.matmul(out[:, HI], wl, moving[:, k, HI], start=False, stop=(k == KD - 1))
                return ins

            def body(e, before, after):
                for j in range(NCH):
                    wait_lo(pe, e, j)
                    wait(pe, summed, NCH * e + j - 1)
                    if j == 0:
                        pe.wait_ge(x_lo, 3 * e + 3)
                    if j == 8:
                        pe.wait_ge(h_lo, 4 * e + 3)
                        product(e, j, range(6))
                        pe.wait_ge(h_lo, 4 * e + 4)
                        ins = product(e, j, range(6, KD))
                    else:
                        ins = product(e, j, range(KD))
                    ins.then_inc(mm5, 1)
                    if before and j in (0, 1):
                        y_back(e - 1, j)
                    if after and j == 9:
                        x_rows(e + 1, 0)
                        x_rows(e + 1, 1)
                    if after and j == 10:
                        x_rows(e + 1, 2)

            pe.wait_ge(tk, 1 + 3 * (ROUNDS_P + ROUNDS_S))
            pe.wait_ge(packed, 1)
            flat = "e k t -> e (k t)"
            for s, at_col, rows in ((0, 0, idx_r[0][:]), (0, 1, gates_r[0][:]), (1, 0, idx_r[1][:]),
                                    (1, 1, gates_w[:].rearrange(flat)), (1, 2, idx_w[:].rearrange(flat))):
                n = rows.shape[-1]
                ins = nc.tensor.transpose(bank[4 + s][0:n, at_col * NEXP:(at_col + 1) * NEXP], rows,
                                          ident[0:NEXP, 0:NEXP])
            ins.then_inc(tk_tr, 1)
            for b in range(3):
                x_rows(0, b)
            run_experts(pe, body)
            for s in range(2):
                y_back(NEXP - 1, s)

    ctx.close()


def kernel(**inputs):
    import numpy as np
    import concourse.bacc as bacc
    from concourse import mybir
    from concourse.bass_utils import run_bass_kernel_spmd

    a = {name: np.asarray(value) for name, value in inputs.items()}
    data = {
        "x": np.concatenate([a["x_prompt"][0], a["x_sample"][0]]),
        "mem": np.concatenate([a["mem_prompt"][0], a["mem_sample"][0]]),
        "g1": a["norm1_g"][0], "gm": a["mem_norm_g"][0], "gq": a["q_norm_g"][0], "gk": a["k_norm_g"][0],
        "gxq": a["xq_norm_g"][0], "gxk": a["xk_norm_g"][0], "convw": a["conv_w"][0],
        "w_in": a["w_in"][0], "w_mem": a["w_mem_kv"][0], "w_bc": a["w_br_conv"][0],
        "w_ba": a["w_br_attn"][0], "w_bx": a["w_br_xattn"][0], "w_o": a["w_o"][0],
        "g2": a["norm2_g"][0], "w_r": a["w_router"][0], "w_eg": a["w_exp_gate"][0],
        "w_eu": a["w_exp_up"][0], "w_ed": a["w_exp_down"][0],
    }
    nc = bacc.Bacc("TRN2", target_bir_lowering=False, num_devices=1)
    arrays, args = {}, {}
    for name, value in data.items():
        value = np.ascontiguousarray(value)
        arrays[f"in_{name}"] = value
        args[name] = nc.dram_tensor(f"in_{name}", value.shape, mybir.dt.from_np(value.dtype),
                                    kind="ExternalInput").ap()
    y = nc.dram_tensor("out_y", (NT, D), F32, kind="ExternalOutput").ap()
    kernel_body(nc, y=y, **args)
    rows = run_bass_kernel_spmd(nc, [arrays], core_ids=[0]).results[0]["out_y"]
    return rows[None, :NP_], rows[None, NP_:]
```
